# Optimizing a Trainium2 kernel written in Bass

```python
import jax, jax.numpy as jnp
from jax import lax
import numpy as np

D_MODEL = 1024
BATCH = 1
SEQ = 256
DEPTH = 2

CTX_LEN = 256
GRID_W = 64
EPS = 1e-6
N_MOD = 9
D_FF = 2816

FNET_GROUPS = 4
FNET_GROUP_DIM = 128
FNET_DIM = FNET_GROUPS * FNET_GROUP_DIM
NA_HEADS = 8
NA_HEAD_DIM = 64
NA_DIM = NA_HEADS * NA_HEAD_DIM
NA_KH = 8
NA_KW = 16
AB_IN_DIM = FNET_DIM + 3 * NA_DIM
AB_OUT_DIM = FNET_DIM + NA_DIM
MLA_HEADS = 8
MLA_NOPE = 128
MLA_ROPE = 64
MLA_V = 128
MLA_Q_RANK = 384
MLA_KV_RANK = 128
MLA_IN_DIM = MLA_Q_RANK + MLA_KV_RANK + MLA_ROPE
ROPE_BASE = 10000.0
Q_BLOCK = 128

N_EVEN = (DEPTH + 1) // 2
N_ODD = DEPTH // 2


def rmsnorm(x, g):
    xf = x.astype(jnp.float32)
    y = xf * lax.rsqrt(jnp.mean(xf * xf, axis=-1, keepdims=True) + EPS)
    return (y * g.astype(jnp.float32)).astype(x.dtype)

def swiglu(h, w_gate, w_up, w_down):
    return (jax.nn.silu(h @ w_gate) * (h @ w_up)) @ w_down

def half_ffn(x, shift, scale, gate, g, w_gate, w_up, w_down):
    h = rmsnorm(x, g) * (1 + scale) + shift
    return x + 0.5 * gate * swiglu(h, w_gate, w_up, w_down)

def axial_rope_tables(n_tok, rot_dim):
    pos = jnp.arange(n_tok)
    row = (pos // GRID_W).astype(jnp.float32)
    col = (pos % GRID_W).astype(jnp.float32)
    half = rot_dim // 2
    inv = ROPE_BASE ** (-jnp.arange(0, half, 2, dtype=jnp.float32) / half)
    ang_r = row[:, None] * inv[None]
    ang_c = col[:, None] * inv[None]
    ang = jnp.concatenate([ang_r, ang_r, ang_c, ang_c], axis=-1)
    return jnp.cos(ang), jnp.sin(ang)

def apply_axial_rope(x, cos, sin):
    xf = x.astype(jnp.float32)
    a, b, cc, d = jnp.split(xf, 4, axis=-1)
    rot = jnp.concatenate([-b, a, -d, cc], axis=-1)
    return (xf * cos + rot * sin).astype(x.dtype)

def fourier_mix(u):
    b, n, _ = u.shape
    ug = u.astype(jnp.float32).reshape(b, n, FNET_GROUPS, FNET_GROUP_DIM)
    f = jnp.fft.fft2(ug, axes=(1, 3), norm="ortho").real
    return f.reshape(b, n, FNET_DIM).astype(u.dtype)

def dense_attention(q, k, v):
    s = jnp.einsum('bqhd,bkhd->bhqk', q, k, preferred_element_type=jnp.float32) * (q.shape[-1] ** -0.5)
    p = jax.nn.softmax(s, axis=-1).astype(v.dtype)
    return jnp.einsum('bhqk,bkhd->bqhd', p, v)

def neighbourhood_attention(q, k, v, k_ctx, v_ctx, rpb):
    b, s, h, dh = q.shape
    rows = s // GRID_W
    kh = min(NA_KH, rows)
    kw = NA_KW
    scale = dh ** -0.5
    qg = q.reshape(b, rows, GRID_W, h, dh)
    kg = k.reshape(b, rows, GRID_W, h, dh)
    vg = v.reshape(b, rows, GRID_W, h, dh)
    cols = jnp.arange(GRID_W)
    col_start = jnp.clip(cols - kw // 2, 0, GRID_W - kw)
    col_idx = col_start[:, None] + jnp.arange(kw)[None, :]
    col_off = col_idx - cols[:, None] + (NA_KW - 1)

    def one_row(r):
        r0 = jnp.clip(r - kh // 2, 0, rows - kh)
        row_off = r0 + jnp.arange(kh) - r + (NA_KH - 1)
        k_band = lax.dynamic_slice_in_dim(kg, r0, kh, axis=1)
        v_band = lax.dynamic_slice_in_dim(vg, r0, kh, axis=1)
        k_win = k_band[:, :, col_idx]
        v_win = v_band[:, :, col_idx]
        qr = lax.dynamic_index_in_dim(qg, r, axis=1, keepdims=False)
        bias = rpb[:, row_off[:, None, None], col_off[None, :, :]]
        bias = jnp.transpose(bias, (0, 2, 1, 3)).reshape(h, GRID_W, kh * kw).astype(jnp.float32)
        s_win = jnp.einsum('bqhd,biqjhd->bhqij', qr, k_win, preferred_element_type=jnp.float32)
        s_win = s_win.reshape(b, h, GRID_W, kh * kw) * scale + bias[None]
        s_ctx = jnp.einsum('bqhd,blhd->bhql', qr, k_ctx, preferred_element_type=jnp.float32) * scale
        p = jax.nn.softmax(jnp.concatenate([s_win, s_ctx], axis=-1), axis=-1).astype(v.dtype)
        p_win = p[..., :kh * kw].reshape(b, h, GRID_W, kh, kw)
        p_ctx = p[..., kh * kw:]
        return (jnp.einsum('bhqij,biqjhd->bqhd', p_win, v_win)
                + jnp.einsum('bhql,blhd->bqhd', p_ctx, v_ctx))

    o = lax.map(one_row, jnp.arange(rows))
    return jnp.transpose(o, (1, 0, 2, 3, 4)).reshape(b, s, h * dh)

def fourier_na_mixer(h_lat, h_ctx, w_in, rpb, w_out, need_ctx_out):
    def split(z):
        u = z[..., :FNET_DIM]
        qkv = z[..., FNET_DIM:].reshape(z.shape[0], z.shape[1], 3, NA_HEADS, NA_HEAD_DIM)
        return u, qkv[:, :, 0], qkv[:, :, 1], qkv[:, :, 2]

    u_l, q_l, k_l, v_l = split(h_lat @ w_in)
    u_c, q_c, k_c, v_c = split(h_ctx @ w_in)
    a_l = fourier_mix(u_l)
    b_l = neighbourhood_attention(q_l, k_l, v_l, k_c, v_c, rpb)
    y_lat = jnp.concatenate([a_l, b_l], axis=-1) @ w_out
    if not need_ctx_out:
        return y_lat, None
    a_c = fourier_mix(u_c)
    b_c = dense_attention(q_c, k_c, v_c).reshape(h_ctx.shape[0], h_ctx.shape[1], NA_DIM)
    y_ctx = jnp.concatenate([a_c, b_c], axis=-1) @ w_out
    return y_lat, y_ctx

def mla_block_attention(q_nope, q_rope, k_nope, k_rope, v):
    b, n, h, _ = q_nope.shape
    nb = n // Q_BLOCK
    scale = (MLA_NOPE + MLA_ROPE) ** -0.5
    qn = q_nope.reshape(b, nb, Q_BLOCK, h, MLA_NOPE).swapaxes(0, 1)
    qr = q_rope.reshape(b, nb, Q_BLOCK, h, MLA_ROPE).swapaxes(0, 1)

    def one_block(args):
        qn_b, qr_b = args
        s = (jnp.einsum('bqhd,bkhd->bhqk', qn_b, k_nope, preferred_element_type=jnp.float32)
             + jnp.einsum('bqhr,bkr->bhqk', qr_b, k_rope, preferred_element_type=jnp.float32)) * scale
        p = jax.nn.softmax(s, axis=-1).astype(v.dtype)
        return jnp.einsum('bhqk,bkhd->bqhd', p, v)

    o = lax.map(one_block, (qn, qr))
    return o.swapaxes(0, 1).reshape(b, n, h * MLA_V)

def mla_mixer(h_lat, h_ctx, w_in, g_q, g_kv, w_uq, w_uk, w_uv, w_o, cos, sin, need_ctx_out):
    def project(hh):
        bb, nn = hh.shape[0], hh.shape[1]
        z = hh @ w_in
        c_q = rmsnorm(z[..., :MLA_Q_RANK], g_q)
        c_kv = rmsnorm(z[..., MLA_Q_RANK:MLA_Q_RANK + MLA_KV_RANK], g_kv)
        k_rope = z[..., MLA_Q_RANK + MLA_KV_RANK:]
        q = (c_q @ w_uq).reshape(bb, nn, MLA_HEADS, MLA_NOPE + MLA_ROPE)
        k_nope = (c_kv @ w_uk).reshape(bb, nn, MLA_HEADS, MLA_NOPE)
        v = (c_kv @ w_uv).reshape(bb, nn, MLA_HEADS, MLA_V)
        return q[..., :MLA_NOPE], q[..., MLA_NOPE:], k_nope, k_rope, v

    qn_l, qr_l, kn_l, kr_l, v_l = project(h_lat)
    qn_c, qr_c, kn_c, kr_c, v_c = project(h_ctx)
    qr_l = apply_axial_rope(qr_l, cos[:, None, :], sin[:, None, :])
    kr_l = apply_axial_rope(kr_l, cos, sin)
    kn_all = jnp.concatenate([kn_l, kn_c], axis=1)
    kr_all = jnp.concatenate([kr_l, kr_c], axis=1)
    v_all = jnp.concatenate([v_l, v_c], axis=1)
    y_lat = mla_block_attention(qn_l, qr_l, kn_all, kr_all, v_all) @ w_o
    if not need_ctx_out:
        return y_lat, None
    y_ctx = mla_block_attention(qn_c, qr_c, kn_c, kr_c, v_c) @ w_o
    return y_lat, y_ctx

def first_inputs(seed: int = 0) -> dict:
    key = jax.random.key(seed)
    ks = jax.random.split(key, 24)
    f32 = jnp.float32

    def nrm(k, shape, std):
        return jax.random.normal(k, shape, f32) * std

    return {
        "x": nrm(ks[0], (BATCH, SEQ, D_MODEL), 1.0),
        "c": nrm(ks[1], (BATCH, D_MODEL), 1.0),
        "ctx": nrm(ks[2], (BATCH, CTX_LEN, D_MODEL), 1.0),
        "c_ctx": nrm(ks[3], (D_MODEL,), 1.0),
        "ada_w": nrm(ks[4], (DEPTH, D_MODEL, N_MOD * D_MODEL), 0.5 * D_MODEL ** -0.5),
        "ada_b": nrm(ks[5], (DEPTH, N_MOD * D_MODEL), 0.02),
        "norm_g": 1.0 + nrm(ks[6], (DEPTH, 3, D_MODEL), 0.02),
        "ffn_w_gate": nrm(ks[7], (DEPTH, 2, D_MODEL, D_FF), D_MODEL ** -0.5),
        "ffn_w_up": nrm(ks[8], (DEPTH, 2, D_MODEL, D_FF), D_MODEL ** -0.5),
        "ffn_w_down": nrm(ks[9], (DEPTH, 2, D_FF, D_MODEL), D_FF ** -0.5),
        "ab_w_in": nrm(ks[10], (N_EVEN, D_MODEL, AB_IN_DIM), D_MODEL ** -0.5),
        "ab_rpb": nrm(ks[11], (N_EVEN, NA_HEADS, 2 * NA_KH - 1, 2 * NA_KW - 1), 0.1),
        "ab_w_out": nrm(ks[12], (N_EVEN, AB_OUT_DIM, D_MODEL), AB_OUT_DIM ** -0.5),
        "mla_w_in": nrm(ks[13], (N_ODD, D_MODEL, MLA_IN_DIM), D_MODEL ** -0.5),
        "mla_g_q": 1.0 + nrm(ks[14], (N_ODD, MLA_Q_RANK), 0.02),
        "mla_g_kv": 1.0 + nrm(ks[15], (N_ODD, MLA_KV_RANK), 0.02),
        "mla_w_uq": nrm(ks[16], (N_ODD, MLA_Q_RANK, MLA_HEADS * (MLA_NOPE + MLA_ROPE)), MLA_Q_RANK ** -0.5),
        "mla_w_uk": nrm(ks[17], (N_ODD, MLA_KV_RANK, MLA_HEADS * MLA_NOPE), MLA_KV_RANK ** -0.5),
        "mla_w_uv": nrm(ks[18], (N_ODD, MLA_KV_RANK, MLA_HEADS * MLA_V), MLA_KV_RANK ** -0.5),
        "mla_w_o": nrm(ks[19], (N_ODD, MLA_HEADS * MLA_V, D_MODEL), (MLA_HEADS * MLA_V) ** -0.5),
        "final_g": 1.0 + nrm(ks[20], (D_MODEL,), 0.02),
    }

def first_block(x, c, ctx, c_ctx, ada_w, ada_b, norm_g, ffn_w_gate, ffn_w_up, ffn_w_down,
              ab_w_in, ab_rpb, ab_w_out, mla_w_in, mla_g_q, mla_g_kv, mla_w_uq, mla_w_uk,
              mla_w_uv, mla_w_o, final_g):
    n_lat = x.shape[1]
    cos, sin = axial_rope_tables(n_lat, MLA_ROPE)
    sc = jax.nn.silu(c)
    scc = jax.nn.silu(c_ctx)
    x_l, x_c = x, ctx
    for layer in range(DEPTH):
        last = layer == DEPTH - 1
        mod_l = (sc @ ada_w[layer] + ada_b[layer]).reshape(-1, N_MOD, D_MODEL)[:, :, None, :]
        mod_c = (scc @ ada_w[layer] + ada_b[layer]).reshape(N_MOD, D_MODEL)

        x_l = half_ffn(x_l, mod_l[:, 0], mod_l[:, 1], mod_l[:, 2], norm_g[layer, 0],
                       ffn_w_gate[layer, 0], ffn_w_up[layer, 0], ffn_w_down[layer, 0])
        x_c = half_ffn(x_c, mod_c[0], mod_c[1], mod_c[2], norm_g[layer, 0],
                       ffn_w_gate[layer, 0], ffn_w_up[layer, 0], ffn_w_down[layer, 0])

        h_l = rmsnorm(x_l, norm_g[layer, 1]) * (1 + mod_l[:, 4]) + mod_l[:, 3]
        h_c = rmsnorm(x_c, norm_g[layer, 1]) * (1 + mod_c[4]) + mod_c[3]
        i = layer // 2
        if layer % 2 == 0:
            y_l, y_c = fourier_na_mixer(h_l, h_c, ab_w_in[i], ab_rpb[i], ab_w_out[i], not last)
        else:
            y_l, y_c = mla_mixer(h_l, h_c, mla_w_in[i], mla_g_q[i], mla_g_kv[i], mla_w_uq[i],
                                 mla_w_uk[i], mla_w_uv[i], mla_w_o[i], cos, sin, not last)
        x_l = x_l + mod_l[:, 5] * y_l

        x_l = half_ffn(x_l, mod_l[:, 6], mod_l[:, 7], mod_l[:, 8], norm_g[layer, 2],
                       ffn_w_gate[layer, 1], ffn_w_up[layer, 1], ffn_w_down[layer, 1])
        if not last:
            x_c = x_c + mod_c[5] * y_c
            x_c = half_ffn(x_c, mod_c[6], mod_c[7], mod_c[8], norm_g[layer, 2],
                           ffn_w_gate[layer, 1], ffn_w_up[layer, 1], ffn_w_down[layer, 1])
    return rmsnorm(x_l, final_g)


DEPTH_2 = 1

ATTN_GROUPS = ((128, 1), (512, 4), (2048, 16))
N_ATTN_GROUPS = 3
HEADS_PER_GROUP = 8
HEAD_DIM_A = 64
ATTN_GROUP_WIDTH = HEADS_PER_GROUP * HEAD_DIM_A
ATTN_QKV_WIDTH = N_ATTN_GROUPS * ATTN_GROUP_WIDTH
DN_HEADS = 8
DN_HEAD_DIM = 128
DN_WIDTH = DN_HEADS * DN_HEAD_DIM
CONV_WIDTH = 4
CHUNK = 64
N_EXPERT_GROUPS = 4
EXPERTS_PER_GROUP = 4
N_EXPERTS = N_EXPERT_GROUPS * EXPERTS_PER_GROUP
TOP_K = 2
D_EXPERT = 256
PLE_DIM = 256
IN_WIDTHS = (3 * ATTN_QKV_WIDTH, 3 * DN_WIDTH, DN_WIDTH, DN_HEADS, DN_HEADS, D_MODEL, D_MODEL)
IN_TOTAL = 3 * ATTN_QKV_WIDTH + 4 * DN_WIDTH + 2 * DN_HEADS + 2 * D_MODEL


def rms_norm(x, gain):
    xf = x.astype(jnp.float32)
    y = xf * lax.rsqrt(jnp.mean(xf * xf, axis=-1, keepdims=True) + EPS)
    return y * gain.astype(jnp.float32)

def l2_norm(x):
    return x * lax.rsqrt(jnp.sum(x * x, axis=-1, keepdims=True) + EPS)

def split_columns(t, widths):
    out, start = [], 0
    for w in widths:
        out.append(t[..., start:start + w])
        start += w
    return out

def dilated_window_attention(q, k, v, window, dilation):
    b, s, h, dh = q.shape
    blk = window // dilation
    span = blk * dilation
    s_pad = -(-s // span) * span
    n_sub = s_pad // dilation
    nblk = n_sub // blk

    def to_blocks(t):
        t = jnp.pad(t, ((0, 0), (0, s_pad - s), (0, 0), (0, 0)))
        t = t.reshape(b, n_sub, dilation, h, dh).transpose(0, 2, 3, 1, 4)
        return t.reshape(b, dilation, h, nblk, blk, dh)

    def with_prev(t):
        prev = jnp.pad(t[:, :, :, :-1], ((0, 0), (0, 0), (0, 0), (1, 0), (0, 0), (0, 0)))
        return jnp.concatenate([prev, t], axis=4)

    qb = to_blocks(q)
    kb = with_prev(to_blocks(k))
    vb = with_prev(to_blocks(v))
    scores = jnp.einsum('brhnqd,brhnkd->brhnqk', qb, kb) * (dh ** -0.5)
    qi = jnp.arange(blk)[:, None]
    kj = jnp.arange(2 * blk)[None, :]
    dist = blk + qi - kj
    band = (dist >= 0) & (dist <= blk)
    has_prev = jnp.arange(nblk)[:, None, None] > 0
    valid = band[None] & (has_prev | (kj >= blk)[None])
    scores = jnp.where(valid, scores, -jnp.inf)
    m = jnp.max(scores, axis=-1, keepdims=True)
    e = jnp.exp(scores - m)
    denom = jnp.sum(e, axis=-1)
    o = jnp.einsum('brhnqk,brhnkd->brhnqd', e, vb) / denom[..., None]
    lse = m[..., 0] + jnp.log(denom)
    o = o.reshape(b, dilation, h, n_sub, dh).transpose(0, 3, 1, 2, 4).reshape(b, s_pad, h, dh)[:, :s]
    lse = lse.reshape(b, dilation, h, n_sub).transpose(0, 3, 1, 2).reshape(b, s_pad, h)[:, :s]
    return o, lse

def causal_short_conv(x, w):
    kw = w.shape[0]
    s = x.shape[1]
    xp = jnp.pad(x, ((0, 0), (kw - 1, 0), (0, 0)))
    y = xp[:, kw - 1:kw - 1 + s] * w[kw - 1]
    for j in range(kw - 1):
        y = y + xp[:, j:j + s] * w[j]
    return jax.nn.silu(y)

def gated_delta_rule(q, k, v, beta, g):
    b, s, h, dk = q.shape
    dv = v.shape[-1]
    n = s // CHUNK

    def chunkify(t):
        return t.reshape(b, n, CHUNK, h, -1).transpose(1, 0, 3, 2, 4)

    qc, kc, vc = chunkify(q), chunkify(k), chunkify(v)
    bc = beta.reshape(b, n, CHUNK, h).transpose(1, 0, 3, 2)
    gcum = jnp.cumsum(g.reshape(b, n, CHUNK, h).transpose(1, 0, 3, 2), axis=-1)
    tril = jnp.tril(jnp.ones((CHUNK, CHUNK), dtype=bool))
    tril_strict = jnp.tril(jnp.ones((CHUNK, CHUNK), dtype=bool), -1)
    decay_mat = jnp.exp(jnp.where(tril, gcum[..., :, None] - gcum[..., None, :], -jnp.inf))
    kbeta = kc * bc[..., None]
    a_mat = jnp.where(tril_strict, jnp.einsum('nbhid,nbhjd->nbhij', kbeta, kc) * decay_mat, 0.0)
    eye = jnp.eye(CHUNK, dtype=jnp.float32)
    t_mat = lax.linalg.triangular_solve(eye + a_mat, jnp.broadcast_to(eye, a_mat.shape),
                                        left_side=True, lower=True, unit_diagonal=True)
    u = jnp.einsum('nbhij,nbhjd->nbhid', t_mat, vc * bc[..., None])
    w = jnp.einsum('nbhij,nbhjd->nbhid', t_mat, kbeta * jnp.exp(gcum)[..., None])
    attn_intra = jnp.where(tril, jnp.einsum('nbhid,nbhjd->nbhij', qc, kc) * decay_mat, 0.0)
    g_last = gcum[..., -1]
    q_dec = qc * jnp.exp(gcum)[..., None]
    k_tail = kc * jnp.exp(g_last[..., None] - gcum)[..., None]

    def step(state, xs):
        qd, ui, wi, ai, gl, kt = xs
        v_new = ui - jnp.einsum('bhcd,bhde->bhce', wi, state)
        o = jnp.einsum('bhcd,bhde->bhce', qd, state) + jnp.einsum('bhij,bhje->bhie', ai, v_new)
        state = state * jnp.exp(gl)[..., None, None] + jnp.einsum('bhcd,bhce->bhde', kt, v_new)
        return state, o

    s0 = jnp.zeros((b, h, dk, dv), jnp.float32)
    _, o = lax.scan(step, s0, (q_dec, u, w, attn_intra, g_last, k_tail))
    return o.transpose(1, 0, 3, 2, 4).reshape(b, s, h, dv)

def hierarchical_moe(hn, w_rg, b_rg, w_re, b_re, w_gate, w_up, w_down):
    bsz, s, d = hn.shape
    t = hn.reshape(-1, d)
    p_group = jax.nn.softmax(t @ w_rg.astype(jnp.float32) + b_rg.astype(jnp.float32), axis=-1)
    g_idx = jnp.argmax(p_group, axis=-1)
    p_g = jnp.take_along_axis(p_group, g_idx[:, None], axis=-1)
    e_logits = (t @ w_re.astype(jnp.float32) + b_re.astype(jnp.float32)).reshape(-1, N_EXPERT_GROUPS, EXPERTS_PER_GROUP)
    sel_logits = jnp.take_along_axis(e_logits, g_idx[:, None, None], axis=1)[:, 0]
    p_exp = jax.nn.softmax(sel_logits, axis=-1)
    top_p, top_i = lax.top_k(p_exp, TOP_K)
    top_p = top_p / jnp.sum(top_p, axis=-1, keepdims=True)
    w_in_group = jnp.sum(jax.nn.one_hot(top_i, EXPERTS_PER_GROUP) * top_p[..., None], axis=1)
    combine = jax.nn.one_hot(g_idx, N_EXPERT_GROUPS)[:, :, None] * (p_g * w_in_group)[:, None, :]
    y = jnp.zeros_like(t)
    for gi in range(N_EXPERT_GROUPS):
        hg = jnp.einsum('td,edf->tef', t, w_gate[gi])
        hu = jnp.einsum('td,edf->tef', t, w_up[gi])
        act = jax.nn.silu(hg) * hu * combine[:, gi, :, None]
        y = y + jnp.einsum('tef,efd->td', act, w_down[gi])
    return y.reshape(bsz, s, d)

def second_inputs(seed: int = 0) -> dict:
    key = jax.random.key(seed)
    ks = jax.random.split(key, 24)
    f32 = jnp.float32

    def nrm(k, shape, scale):
        return jax.random.normal(k, shape, f32) * scale

    def gain(k, n):
        return 1.0 + 0.05 * jax.random.normal(k, (DEPTH_2, n), f32)

    a_init = jax.random.uniform(ks[6], (DEPTH_2, DN_HEADS), f32, 1.0, 16.0)
    dt = jnp.exp(jax.random.uniform(ks[7], (DEPTH_2, DN_HEADS), f32, float(np.log(1e-3)), float(np.log(1e-1))))
    dt_bias = dt + jnp.log(-jnp.expm1(-dt))
    return {
        "x": nrm(ks[0], (BATCH, SEQ, D_MODEL), 1.0),
        "p": nrm(ks[1], (DEPTH_2, BATCH, SEQ, PLE_DIM), 1.0),
        "norm_mix": gain(ks[2], D_MODEL),
        "w_in": nrm(ks[3], (DEPTH_2, D_MODEL, IN_TOTAL), D_MODEL ** -0.5),
        "q_norm": gain(ks[4], HEAD_DIM_A),
        "k_norm": gain(ks[5], HEAD_DIM_A),
        "conv_w": nrm(ks[8], (DEPTH_2, CONV_WIDTH, 3 * DN_WIDTH), CONV_WIDTH ** -0.5),
        "a_log": jnp.log(a_init),
        "dt_bias": dt_bias,
        "dn_out_norm": gain(ks[9], DN_HEAD_DIM),
        "w_branch_a": nrm(ks[10], (DEPTH_2, ATTN_GROUP_WIDTH, D_MODEL), ATTN_GROUP_WIDTH ** -0.5),
        "w_branch_b": nrm(ks[11], (DEPTH_2, DN_WIDTH, D_MODEL), DN_WIDTH ** -0.5),
        "w_out": nrm(ks[12], (DEPTH_2, D_MODEL, D_MODEL), D_MODEL ** -0.5),
        "norm_ffn": gain(ks[13], D_MODEL),
        "w_router_group": nrm(ks[14], (DEPTH_2, D_MODEL, N_EXPERT_GROUPS), D_MODEL ** -0.5),
        "b_router_group": nrm(ks[15], (DEPTH_2, N_EXPERT_GROUPS), 0.01),
        "w_router_expert": nrm(ks[16], (DEPTH_2, D_MODEL, N_EXPERTS), D_MODEL ** -0.5),
        "b_router_expert": nrm(ks[17], (DEPTH_2, N_EXPERTS), 0.01),
        "w_expert_gate": nrm(ks[18], (DEPTH_2, N_EXPERT_GROUPS, EXPERTS_PER_GROUP, D_MODEL, D_EXPERT), D_MODEL ** -0.5),
        "w_expert_up": nrm(ks[19], (DEPTH_2, N_EXPERT_GROUPS, EXPERTS_PER_GROUP, D_MODEL, D_EXPERT), D_MODEL ** -0.5),
        "w_expert_down": nrm(ks[20], (DEPTH_2, N_EXPERT_GROUPS, EXPERTS_PER_GROUP, D_EXPERT, D_MODEL), D_EXPERT ** -0.5),
        "norm_ple": gain(ks[21], D_MODEL),
        "w_ple": nrm(ks[22], (DEPTH_2, PLE_DIM, D_MODEL), PLE_DIM ** -0.5),
        "w_ple_gate": nrm(ks[23], (DEPTH_2, D_MODEL, D_MODEL), D_MODEL ** -0.5),
    }

def second_block(x, p, norm_mix, w_in, q_norm, k_norm, conv_w, a_log, dt_bias, dn_out_norm,
              w_branch_a, w_branch_b, w_out, norm_ffn, w_router_group, b_router_group,
              w_router_expert, b_router_expert, w_expert_gate, w_expert_up, w_expert_down,
              norm_ple, w_ple, w_ple_gate):
    b, s, d = x.shape
    x = x.astype(jnp.float32)
    for i in range(DEPTH_2):
        h = rms_norm(x, norm_mix[i])
        proj = h @ w_in[i].astype(jnp.float32)
        qkv_a, qkv_b, z_b, beta_b, alpha_b, gate_a, gate_b = split_columns(proj, IN_WIDTHS)

        qkv_a = qkv_a.reshape(b, s, 3, N_ATTN_GROUPS, HEADS_PER_GROUP, HEAD_DIM_A)
        qa = rms_norm(qkv_a[:, :, 0], q_norm[i])
        ka = rms_norm(qkv_a[:, :, 1], k_norm[i])
        va = qkv_a[:, :, 2]
        outs, lses = [], []
        for gi, (win, dil) in enumerate(ATTN_GROUPS):
            o_g, lse_g = dilated_window_attention(qa[:, :, gi], ka[:, :, gi], va[:, :, gi], win, dil)
            outs.append(o_g)
            lses.append(lse_g)
        mix_w = jax.nn.softmax(jnp.stack(lses, axis=0), axis=0)
        o_a = jnp.sum(mix_w[..., None] * jnp.stack(outs, axis=0), axis=0).reshape(b, s, ATTN_GROUP_WIDTH)

        qkv_b = causal_short_conv(qkv_b, conv_w[i].astype(jnp.float32))
        qb, kb, vb = split_columns(qkv_b, (DN_WIDTH, DN_WIDTH, DN_WIDTH))
        qb = l2_norm(qb.reshape(b, s, DN_HEADS, DN_HEAD_DIM)) * (DN_HEAD_DIM ** -0.5)
        kb = l2_norm(kb.reshape(b, s, DN_HEADS, DN_HEAD_DIM))
        vb = vb.reshape(b, s, DN_HEADS, DN_HEAD_DIM)
        beta = jax.nn.sigmoid(beta_b)
        g = -jnp.exp(a_log[i].astype(jnp.float32)) * jax.nn.softplus(alpha_b + dt_bias[i].astype(jnp.float32))
        o_b = gated_delta_rule(qb, kb, vb, beta, g)
        o_b = rms_norm(o_b, dn_out_norm[i]) * jax.nn.silu(z_b.reshape(b, s, DN_HEADS, DN_HEAD_DIM))
        o_b = o_b.reshape(b, s, DN_WIDTH)

        merged = (jax.nn.sigmoid(gate_a) * (o_a @ w_branch_a[i].astype(jnp.float32))
                  + jax.nn.sigmoid(gate_b) * (o_b @ w_branch_b[i].astype(jnp.float32)))
        x = x + merged @ w_out[i].astype(jnp.float32)

        h2 = rms_norm(x, norm_ffn[i])
        x = x + hierarchical_moe(h2, w_router_group[i], b_router_group[i], w_router_expert[i],
                                 b_router_expert[i], w_expert_gate[i].astype(jnp.float32),
                                 w_expert_up[i].astype(jnp.float32), w_expert_down[i].astype(jnp.float32))

        h3 = rms_norm(x, norm_ple[i])
        ple = p[i].astype(jnp.float32) @ w_ple[i].astype(jnp.float32)
        x = x + jax.nn.sigmoid(h3 @ w_ple_gate[i].astype(jnp.float32)) * ple
    return x


def setup_inputs(seed=0):
    out = dict(first_inputs(seed))
    for name, value in second_inputs(seed + 1).items():
        if name != "x":
            out[name + "_2"] = value
    return out


def reference(
    x, c, ctx, c_ctx, ada_w, ada_b, norm_g, ffn_w_gate, ffn_w_up, ffn_w_down, ab_w_in, ab_rpb,
    ab_w_out, mla_w_in, mla_g_q, mla_g_kv, mla_w_uq, mla_w_uk, mla_w_uv, mla_w_o, final_g, p_2,
    norm_mix_2, w_in_2, q_norm_2, k_norm_2, conv_w_2, a_log_2, dt_bias_2, dn_out_norm_2,
    w_branch_a_2, w_branch_b_2, w_out_2, norm_ffn_2, w_router_group_2, b_router_group_2,
    w_router_expert_2, b_router_expert_2, w_expert_gate_2, w_expert_up_2, w_expert_down_2,
    norm_ple_2, w_ple_2, w_ple_gate_2,
):
    x = first_block(
        x, c, ctx, c_ctx, ada_w, ada_b, norm_g, ffn_w_gate, ffn_w_up, ffn_w_down, ab_w_in,
        ab_rpb, ab_w_out, mla_w_in, mla_g_q, mla_g_kv, mla_w_uq, mla_w_uk, mla_w_uv, mla_w_o,
        final_g,
    )
    return second_block(
        x, p_2, norm_mix_2, w_in_2, q_norm_2, k_norm_2, conv_w_2, a_log_2, dt_bias_2,
        dn_out_norm_2, w_branch_a_2, w_branch_b_2, w_out_2, norm_ffn_2, w_router_group_2,
        b_router_group_2, w_router_expert_2, b_router_expert_2, w_expert_gate_2, w_expert_up_2,
        w_expert_down_2, norm_ple_2, w_ple_2, w_ple_gate_2,
    )


_drawn_inputs = setup_inputs


def setup_inputs(seed=0):
    import zlib

    import numpy as np

    out = dict(_drawn_inputs(seed))
    spreads = {}
    factors = {'norm_g': 3.672,
     'ab_rpb': 8.0,
     'mla_g_q': 8.0,
     'mla_g_kv': 8.0,
     'q_norm_2': 5.176,
     'k_norm_2': 8.0,
     'dn_out_norm_2': 2.88,
     'b_router_group_2': 5.364,
     'b_router_expert_2': 8.0,
     'norm_ple_2': 18.278}
    for name, (base, spread) in spreads.items():
        noise = np.random.default_rng([zlib.crc32(name.encode()), seed]).standard_normal(out[name].shape)
        drawn = base * np.exp(spread * noise) if base else spread * noise
        out[name] = __import__('jax').numpy.asarray(drawn.astype(out[name].dtype))
    for name, factor in factors.items():
        out[name] = (out[name] * factor).astype(out[name].dtype)
    return out
```

```python
from contextlib import ExitStack, contextmanager

import numpy as np

import concourse.bass as bass
from concourse import mybir

F32 = mybir.dt.float32
F32R = mybir.dt.float32r
ALU = mybir.AluOpType
ACT = mybir.ActivationFunctionType
AX = mybir.AxisListType

P = 128
D = 1024
KT = D // P
SEQ = 256
TOK = 2 * SEQ
QT = SEQ // P
N_MOD = 9
FF_TILES = 2816 // P
N_EXPERTS = 16
EXP_TILES = N_EXPERTS * 2
EPS = 1e-6
NEG = -1e30
UNIT = 8 * P
SLOTS = 4
LOOK = 2

NA_SCALE = 64 ** -0.5
MLA_SCALE = 192 ** -0.5

STREAM = [
    ("ada", 144, UNIT, (18, 18, 0, 0)),
    ("up0", 44, UNIT, (11, 11, 11, 11)), ("down0", 24, UNIT, (2, 2, 2, 2)),
    ("ab_uqk", 12, UNIT, (3, 3, 3, 3)), ("ab_v", 4, UNIT, (1, 1, 1, 1)),
    ("ab_out", 8, UNIT, (2, 2, 2, 2)),
    ("up1", 44, UNIT, (11, 11, 11, 11)), ("down1", 24, UNIT, (2, 2, 2, 2)),
    ("up2", 44, UNIT, (11, 11, 11, 11)), ("down2", 24, UNIT, (2, 2, 2, 2)),
    ("mla_in", 5, UNIT, (2, 1, 1, 1)), ("mla_uq", 6, 6 * P, (3, 3, 3, 3)),
    ("mla_uk", 2, 4 * P, (2, 2, 2, 2)), ("mla_uv", 2, 4 * P, (2, 2, 2, 2)),
    ("mla_o", 8, UNIT, (2, 2, 2, 2)),
    ("up3", 44, UNIT, (11, 11, 11, 11)), ("down3", 24, UNIT, (2, 2, 2, 2)),
    ("b_qk", 24, UNIT, (6, 6, 6, 6)), ("b_v", 12, UNIT, (2, 2, 1, 1)),
    ("b_conv", 24, UNIT, (6, 6, 6, 6)), ("b_z", 8, UNIT, (2, 2, 2, 2)),
    ("b_gates", 16, UNIT, (4, 4, 4, 4)),
    ("branch_a", 4, UNIT, (2, 2, 2, 2)), ("branch_b", 8, UNIT, (2, 2, 2, 2)),
    ("b_out", 8, UNIT, (2, 2, 2, 2)),
    ("exp_up", 64, UNIT, (16, 16, 16, 16)), ("exp_down", 32, UNIT, (2, 2, 2, 2)),
    ("ple_gate", 8, UNIT, (2, 2, 2, 2)), ("ple_w", 2, UNIT, (2, 2, 2, 2)),
]
SIZES = {name: n for name, _, n, _ in STREAM}
FIRST, COUNT, READS = {}, {}, {}
_u, _r = 0, (1, 1, 1, 1)
for _name, _n, _, _g in STREAM:
    FIRST[_name], COUNT[_name], READS[_name] = _u, _n, _r
    _u, _r = _u + _n, tuple(a + b for a, b in zip(_r, _g))
    READS[_name + " end"] = _r
SPLIT0 = COUNT["ada"]

PARAMS = [
    ("cond", KT * 2), ("ada_b", 2 * N_MOD * KT), ("norm_g", 6 * KT), ("final_g", KT), ("g_q", 3), ("g_kv", 1),
    ("norm_mix", KT), ("q_norm", 1), ("k_norm", 1), ("conv_w", 24 * 4), ("dn_norm", 1), ("norm_ffn", KT),
    ("norm_ple", KT), ("a_log", 8), ("dt_bias", 8), ("b_router", 20),
]
PCOL, _c = {}, 0
for _name, _n in PARAMS:
    PCOL[_name] = (_c, _c + _n)
    _c += _n
NPAR = _c


class Tally:

    def __init__(self, sem, start=0):
        self.sem, self.base, self.k = sem, start, 0

    def inc(self, ins):
        ins.then_inc(self.sem, 1)
        self.k += 1
        return self.base + self.k

    @property
    def value(self):
        return self.base + self.k


@contextmanager
def counted(eng, n, *tallies):
    starts = [t.value for t, _ in tallies]
    with eng.Fori(0, n) as i:
        for (t, per), s in zip(tallies, starts):
            t.base, t.k = i * per + s, 0
        yield i
        for t, per in tallies:
            assert t.k == per, (t.k, per)
    for (t, per), s in zip(tallies, starts):
        t.base, t.k = s + n * per, 0


def host_constants():
    i = np.arange(P)
    eye = np.eye(P)
    half = (i[:, None] // 64 == i[None, :] // 64).astype(float)
    base = np.concatenate([eye, np.ones((P, P)), half], 1)

    ang_d = 2 * np.pi * (np.outer(i, i) % P) / P
    n = np.arange(SEQ)
    ang_n = 2 * np.pi * (np.outer(n, n) % SEQ) / SEQ
    s = (P * SEQ) ** -0.5
    cn, sn = np.cos(ang_n) * s, -np.sin(ang_n) * s
    tile = lambda a: a.reshape(QT, P, SEQ).transpose(1, 0, 2).reshape(P, QT * SEQ)
    dft = np.concatenate([np.cos(ang_d), np.sin(ang_d), tile(cn), tile(sn)], 1)

    inv = 10000.0 ** (-np.arange(0, 32, 2, dtype=np.float32) / 32)
    ar, ac = (n // 64)[:, None] * inv[None], (n % 64)[:, None] * inv[None]
    ang = np.concatenate([ar, ar, ac, ac], -1).astype(np.float32)
    rot = np.zeros((64, 64))
    for b in (0, 32):
        for j in range(16):
            rot[b + 16 + j, b + j] = -1.0
            rot[b + j, b + 16 + j] = 1.0
    rot2 = np.zeros((P, P))
    rot2[:64, :64] = rot2[64:, 64:] = rot
    rope = np.concatenate([rot2, np.tile(np.cos(ang).T, (2, 1)), np.tile(np.sin(ang).T, (2, 1))], 1)

    t, k = np.arange(SEQ)[:, None], np.arange(SEQ)[None, :]
    ok = [(k <= t) & ((t - k) % dil == 0) & (t - k <= win) for win, dil in ((128, 1), (512, 4), (2048, 16))]
    add = [np.where(o, 0.0, NEG) for o in ok]
    bands = np.concatenate([a[:P, :P] for a in add] + [a[P:] for a in add], 1)

    utri = (i[:, None] <= i[None, :]).astype(float)
    low = np.where(i[None, :] <= i[:, None], 0.0, -NEG)
    up = np.where(i[None, :] >= i[:, None], 0.0, NEG)
    levels = []
    for b in range(7):
        s = 1 << b
        levels.append(((i[:, None] // (2 * s) == i[None, :] // (2 * s))
                       & (i[:, None] % (2 * s) >= s) & (i[None, :] % (2 * s) < s)).astype(float))
    delta = np.concatenate([utri, low, up] + levels, 1)
    desc = np.tile(np.arange(4, 0, -1.0), (P, 1))
    return {k: np.ascontiguousarray(v, np.float32) for k, v in
            dict(c_base=base, c_dft=dft, c_rope=rope, c_bands=bands, c_delta=delta, c_desc=desc).items()}


def window_layout():
    q, k = np.arange(SEQ)[:, None], np.arange(SEQ)[None, :]
    r, c, i, j = q // 64, q % 64, k // 64, k % 64
    start = np.clip(c - 8, 0, 48)
    inside = (j >= start) & (j < start + 16)
    return i - r + 7, np.where(inside, j - c + 15, 0), inside


def chunk_maker(inputs):
    def fm(w, kt=KT):
        K, N = w.shape
        return w.reshape(K // P, P, N // P, P).transpose(2, 1, 0, 3)

    def units(w):
        return np.ascontiguousarray(fm(w)).reshape(w.shape[1] // P, P, -1)

    def moving(w, nb=512, kk=2):
        K, N = w.shape
        a = w.reshape(K // P // kk, kk, P, N // nb, nb).transpose(3, 0, 2, 1, 4)
        return np.ascontiguousarray(a).reshape(-1, P, kk * nb)

    def up(g, u):
        a = np.stack([fm(g), fm(u)], 1)
        return np.ascontiguousarray(a).reshape(-1, P, UNIT)

    def down(w):
        a = fm(w)
        n, _, kt, _ = a.shape
        per = -(-kt // 8)
        out = np.zeros((n, per, P, 8, P), w.dtype)
        for j in range(per):
            m = min(8, kt - 8 * j)
            out[:, j, :, :m] = a[:, :, 8 * j:8 * j + m]
        return out.reshape(n * per, P, UNIT)

    def pack(w, per):
        a = fm(w)
        n, _, kt, _ = a.shape
        a = a.reshape(n // per, per, P, kt, P).transpose(0, 2, 1, 3, 4)
        return np.ascontiguousarray(a).reshape(n // per, P, per * kt * P)

    f = inputs
    w_in = f["w_in_2"][0]
    ab, ml = f["ab_w_in"][0], f["mla_w_in"][0]
    rope_w = ml[:, 512:]
    uq = f["mla_w_uq"][0].reshape(384, 8, 192)
    uq = np.concatenate([uq[:, :, :128].reshape(384, 1024), uq[:, :, 128:].reshape(384, 512)], 1)
    eg = f["w_expert_gate_2"][0].reshape(16, D, 256).transpose(1, 0, 2).reshape(D, 4096)
    eu = f["w_expert_up_2"][0].reshape(16, D, 256).transpose(1, 0, 2).reshape(D, 4096)
    out = {
        "ada": np.concatenate([moving(f["ada_w"][l]) for l in range(2)]),
        "ab_uqk": units(ab[:, :1536]), "ab_v": moving(ab[:, 1536:]), "ab_out": units(f["ab_w_out"][0]),
        "mla_in": units(np.concatenate([ml, rope_w], 1)),
        "mla_uq": pack(uq, 2), "mla_uk": pack(f["mla_w_uk"][0], 4), "mla_uv": moving(f["mla_w_uv"][0], 512, 1),
        "mla_o": units(f["mla_w_o"][0]),
        "b_qk": units(w_in[:, :3072]), "b_v": moving(w_in[:, 3072:4608]), "b_conv": units(w_in[:, 4608:7680]),
        "b_z": units(w_in[:, 7680:8704]), "b_gates": units(w_in[:, 8720:]),
        "branch_a": pack(f["w_branch_a_2"][0], 2), "branch_b": units(f["w_branch_b_2"][0]),
        "b_out": units(f["w_out_2"][0]),
        "exp_up": up(eg, eu), "exp_down": down(f["w_expert_down_2"][0].reshape(4096, D)),
        "ple_gate": units(f["w_ple_gate_2"][0]), "ple_w": pack(f["w_ple_2"][0], 4),
    }
    for n in range(4):
        out[f"up{n}"] = up(f["ffn_w_gate"][n // 2, n % 2], f["ffn_w_up"][n // 2, n % 2])
        out[f"down{n}"] = down(f["ffn_w_down"][n // 2, n % 2])
    return {k: v.reshape(COUNT[k], P, SIZES[k]) for k, v in out.items()}


def host_inputs(inputs):
    f = {k: np.asarray(v) for k, v in inputs.items()}
    cols = lambda v: v.reshape(-1, P).T
    feat = lambda a: a.T.reshape(-1, P, a.shape[0]).transpose(1, 0, 2)
    rows = lambda v: np.broadcast_to(v.reshape(1, -1), (P, v.size))
    cond = np.stack([cols(f["c"][0]), cols(f["c_ctx"])], 2).reshape(P, -1)
    conv = f["conv_w_2"][0].T.reshape(24, P, 4).transpose(1, 0, 2).reshape(P, -1)
    dup = lambda v: np.concatenate([v, v]).reshape(P, 1)
    params = {
        "cond": cond, "ada_b": cols(f["ada_b"].reshape(-1)), "norm_g": cols(f["norm_g"].reshape(-1)),
        "final_g": cols(f["final_g"]), "g_q": cols(f["mla_g_q"][0]), "g_kv": cols(f["mla_g_kv"][0]),
        "norm_mix": cols(f["norm_mix_2"][0]), "q_norm": dup(f["q_norm_2"][0]), "k_norm": dup(f["k_norm_2"][0]),
        "conv_w": conv, "dn_norm": cols(f["dn_out_norm_2"][0]), "norm_ffn": cols(f["norm_ffn_2"][0]),
        "norm_ple": cols(f["norm_ple_2"][0]), "a_log": rows(f["a_log_2"][0]), "dt_bias": rows(f["dt_bias_2"][0]),
        "b_router": rows(np.concatenate([f["b_router_group_2"][0], f["b_router_expert_2"][0]])),
    }
    x = np.concatenate([feat(f["x"][0]), feat(f["ctx"][0])], 2)
    ri, ci, inside = window_layout()
    bias = np.where(inside, f["ab_rpb"][0][:, ri, ci], np.float32(NEG))
    bias = bias.reshape(8, QT, P, SEQ).transpose(2, 0, 1, 3)
    tall = lambda w: w.reshape(KT, P, -1).transpose(1, 0, 2).reshape(P, -1)
    w_small = np.concatenate([tall(f["w_in_2"][0][:, 8704:8720]), tall(np.concatenate(
        [f["w_router_group_2"][0], f["w_router_expert_2"][0]], 1))], 1)
    out = {"w_" + k: v for k, v in chunk_maker(f).items()}
    out.update(host_constants())
    out.update(params=np.concatenate([params[n] for n, _ in PARAMS], 1), x_t=x, bias=bias,
               ple=feat(f["p_2"][0, 0]), w_small=w_small)
    return {k: np.ascontiguousarray(v) for k, v in out.items()}

PHASES = ["ada", "ffn0", "mixer_a", "ffn1", "ffn2", "mla", "ffn3", "final", "attn_b", "delta", "merge", "moe", "ple"]


def build_program(nc, dram, out, last_phase="ple"):
    ctx = ExitStack()
    phases = PHASES[:PHASES.index(last_phase) + 1]
    with ctx:
        def sb(name, shape, dt=F32):
            return ctx.enter_context(nc.sbuf_tensor(name, shape, dt))

        def sem(name):
            return ctx.enter_context(nc.semaphore(name))

        x = sb("x", [P, KT, TOK])
        raw = [sb(f"raw{s}", [P, UNIT]) for s in range(SLOTS)]
        whi = [sb(f"whi{s}", [P, UNIT], F32R) for s in range(SLOTS)]
        wlo = [sb(f"wlo{s}", [P, UNIT], F32R) for s in range(SLOTS)]
        H = KT * TOK
        A = FF_TILES * TOK
        h_at = nc.sbuf_base
        h_all = sb("h_all", [P, 2 * H], F32R)
        a_at = nc.sbuf_base
        a_all = sb("a_all", [P, 2 * A], F32R)
        assert h_at % 32 == 0 and a_at == h_at + 8 * H and nc.sbuf_base == a_at + 8 * A
        base = sb("base", [P, 3 * P])
        par = sb("par", [P, NPAR])
        gbuf = [sb(f"gbuf{j}", [P, TOK]) for j in range(2)]
        std = [sb(f"std{j}", [P, TOK]) for j in range(2)]
        sqb = gbuf
        small_hi, small_lo = sb("small_hi", [P, 288], F32R), sb("small_lo", [P, 288], F32R)
        mods = sb("mods", [P, 2 * N_MOD * KT, 2])
        gains = sb("gains", [P, 6, KT, 2])
        cond = sb("cond", [P, KT, 2])
        eps = sb("eps", [P, 1])
        small = sb("small", [P, 512])
        ident, ones, half_ones = base[:, 0:P], base[:, P:2 * P], base[:, 2 * P:3 * P]

        work = nc.alloc_sbuf_tensor_at("work", [P, 2 * A], F32, offset=a_at)
        hwork = nc.alloc_sbuf_tensor_at("hwork", [P, 2 * H], F32, offset=h_at)

        def W(at, *shape):
            n = int(np.prod(shape))
            return view(work[:, at:at + n], shape)

        def R(at, *shape):
            n = int(np.prod(shape))
            return view(a_all[:, at:at + n], shape)

        def view(ap, shape):
            if len(shape) == 1:
                return ap
            if len(shape) == 2:
                return ap.rearrange("p (a b) -> p a b", a=shape[0])
            return ap.rearrange("p (a b c) -> p a b c", a=shape[0], b=shape[1])

        h_hi, h_lo = (view(h_all[:, j * H:(j + 1) * H], (KT, TOK)) for j in range(2))
        a_hi, a_lo = (view(a_all[:, j * A:(j + 1) * A], (FF_TILES, TOK)) for j in range(2))
        EA = EXP_TILES * SEQ
        e_hi, e_lo = R(0, EXP_TILES, SEQ), R(EA, EXP_TILES, SEQ)
        combine_rows = W(2 * EA, N_EXPERTS, SEQ)

        def P_(name):
            a, b = PCOL[name]
            return par[:, a:b]

        lin = ctx.enter_context(nc.psum_tensor("lin", [P, 4, 512], F32))
        pair = [ctx.enter_context(nc.psum_tensor(f"pair{j}", [P, 2, 512], F32)) for j in range(2)]
        norm_bank = pair[1][:, 1]

        raw_loaded = [sem(f"raw_loaded{s}") for s in range(SLOTS)]
        weights_split = sem("weights_split")
        units_done = sem("units_done")
        lin_read = [sem(f"lin_read{b}") for b in range(4)]
        inner_ready = sem("inner_ready")
        vec, act_own = sem("vector_step"), sem("scalar_step")
        made = {}

        def S(name):
            if name not in made:
                made[name] = sem(name)
            return made[name]

        A_U, A_Q, A_K, A_V = (j * 2048 for j in range(4))
        A_DFT, A_BIAS, A_FV, A_P, A_PT, A_CAT = 8192, 9472, 13568, 14592, 15616, 16640
        M_CQ, M_CKV, M_KR, M_QR = 0, 768, 1280, 1792
        M_CQH, M_CQL, M_CKH, M_CKL = 2816, 3584, 4352, 4864
        M_KRR, M_QRR, M_QN, M_KN, M_V, M_P, M_PT, M_ROPE, M_O = (
            5376, 5888, 6912, 8960, 13056, 17152, 18176, 19200, 19840)
        B_QK, B_V, B_BANDS, B_P, B_PT, B_OA = 0, 6144, 9216, 10368, 11904, 13440
        OA_HI, OA_LO = 20480, 21504
        D_CV, D_Z, D_A, D_T, D_TT, D_Q1, D_AT, D_TMP = 0, 6144, 8192, 10240, 12288, 14336, 16384, 18432
        C_GATE, C_M, C_MH, C_ML, OB_HI, OB_LO = 10240, 14336, 16384, 18432, 0, 2048

        h_wide = view(hwork[:, 0:H], (KT, TOK))

        def delta_table(n):
            return h_wide[:, n // 2, SEQ + (n % 2) * P:SEQ + (n % 2 + 1) * P]


        def softmax_items(kind):
            items = []
            for h in range(8):
                half, t2 = slice(64 * (h % 2), 64 * (h % 2) + 64), h // 2
                for qt in range(QT):
                    q0 = qt * P
                    if kind == "window":
                        q, k, v = W(A_Q, 4, TOK), W(A_K, 4, TOK), W(A_V, 4, 512)
                        bias = W(A_BIAS, 8, QT * SEQ)[:, h, qt * SEQ:(qt + 1) * SEQ]
                        items.append(([(0, 512, q[half, t2, q0:q0 + P], k[half, t2, :]), (0, SEQ, ident, bias)],
                                      512, 1.0, [v[:, kt, 64 * h:64 * h + 64] for kt in range(4)],
                                      W(A_CAT, KT, TOK)[half, 4 + t2, q0:q0 + P], half))
                    if kind == "context":
                        q, k, v = W(A_Q, 4, TOK), W(A_K, 4, TOK), W(A_V, 4, 512)
                        items.append(([(0, SEQ, q[half, t2, SEQ + q0:SEQ + q0 + P], k[half, t2, SEQ:TOK])],
                                      SEQ, 1.0, [v[:, kt, 64 * h:64 * h + 64] for kt in (2, 3)],
                                      W(A_CAT, KT, TOK)[half, 4 + t2, SEQ + q0:SEQ + q0 + P], half))
                    if kind == "mla":
                        qn, qr = W(M_QN, 8, SEQ), W(M_QRR, 4, SEQ)
                        kn, kr, v = W(M_KN, 8, TOK), W(M_KRR, TOK), W(M_V, 4, 1024)
                        items.append(([(0, 512, qn[:, h, q0:q0 + P], kn[:, h, :]),
                                       (0, 512, qr[half, t2, q0:q0 + P], kr[half, :])],
                                      512, MLA_SCALE, [v[:, kt, P * h:P * h + P] for kt in range(4)],
                                      W(M_O, 8, SEQ)[:, h, q0:q0 + P], slice(0, P)))
                    if kind == "banded":
                        qk, v, n = W(B_QK, 24, SEQ), W(B_V, QT, 1536), P * (qt + 1)
                        bands = work[:, B_BANDS + 384 * qt:B_BANDS + 384 * qt + 3 * n]
                        ops = [(0, 384, ident, bands)] if qt == 0 else [
                            (0, 512, ident, bands[:, 0:512]), (512, 768, ident, bands[:, 512:768])]
                        for g in range(3):
                            ops.append((g * n, (g + 1) * n, qk[half, 4 * g + t2, q0:q0 + P], qk[half, 12 + 4 * g + t2, 0:n]))
                        items.append((ops, 3 * n, NA_SCALE,
                                      [v[:, kt, 512 * g + 64 * h:512 * g + 64 * h + 64]
                                       for g in range(3) for kt in range(qt + 1)],
                                      W(B_OA, 4, SEQ)[half, t2, q0:q0 + P], half))
            return items

        def group_norms(kind):
            items = []
            if kind == "mla":
                cq, ck = W(M_CQ, 3, SEQ), W(M_CKV, TOK)
                items.append(([cq[:, k] for k in range(3)], ones, 1 / 384,
                              [(cq[:, k], P_("g_q")[:, k:k + 1], cq[:, k]) for k in range(3)]))
                items.append(([ck], ones, 1 / 128, [(ck, P_("g_kv"), ck)]))
            if kind == "qk":
                for n in range(12):
                    qk = W(B_QK, 12, 512)[:, n]
                    items.append(([qk], half_ones, 1 / 64, [(qk, P_("q_norm" if n < 6 else "k_norm"), qk)]))
            if kind == "delta":
                for n in range(8):
                    t = W(D_CV, 12, 512)[:, n]
                    items.append(([t], ones, 1.0, [(t, P ** -0.5 if n < 4 else 1.0, t)]))
            if kind == "delta_out":
                for n in range(4):
                    t = W(D_CV + 4096, 4, 512)[:, n]
                    items.append(([t], ones, 1 / 128, [(t, P_("dn_norm"), t)]))
            return items

        NORMS = {
            "ffn0": (0, TOK, "load"), "mixer_a": (1, TOK, "down0"), "ffn1": (2, TOK, "ab_out"),
            "ffn2": (3, TOK, "down1"), "mla": (4, TOK, "down2"), "ffn3": (5, SEQ, "mla_o"),
            "final": (6, SEQ, "down3"), "attn_b": (7, SEQ, "final"), "moe": (8, SEQ, "b_out"),
            "ple": (9, SEQ, "exp_down"),
        }

        def squares_of(phase):
            return W(4096, KT, TOK) if NORMS[phase][2] in ("ab_out", "mla_o", "b_out") else h_wide

        def norm_gain(phase, k, s):
            if phase in ("ffn0", "mixer_a", "ffn1", "ffn2", "mla", "ffn3"):
                return gains[:, NORMS[phase][0], k, s:s + 1]
            name = {"final": "final_g", "attn_b": "norm_mix", "moe": "norm_ffn", "ple": "norm_ple"}[phase]
            return P_(name)[:, k:k + 1]

        def mod(layer, m, k, s):
            return mods[:, layer * 72 + m * 8 + k, s:s + 1]

        def body(stage):
            return 12 if stage.startswith("down") else 16 if stage == "exp_down" else 4

        def width(stage, j):
            return 6 * P if stage.startswith("down") and j % 3 == 2 else SIZES[stage]


        beta, alpha, minus_abs, soft, decay_rate, gate = (
            view(small[:, 32:48], (2, 8)), view(small[:, 48:64], (2, 8)), view(small[:, 64:80], (2, 8)),
            view(small[:, 80:96], (2, 8)), small[:, 96:104], view(small[:, 112:128], (2, 8)))
        cum, minus_cum, tail, grown, minus_grown = (
            view(small[:, 128:144], (2, 8)), view(small[:, 144:160], (2, 8)), small[:, 160:168],
            small[:, 168:176], small[:, 176:184])
        v_rows = view(hwork[:, H:2 * H], (KT, TOK))[:, :, SEQ:TOK]
        k_tail = W(15360, 8, P)
        inv, inv_t, lower = W(D_T, 16, P), W(D_TT, 16, P), W(D_A, 16, P)
        attn_t = W(D_AT, 16, P)
        new_v, state, mixed = W(D_A, 16, P), W(D_T, 8, P), W(D_T + 1024, 8, P)
        LEVELS = 7

        def wide(ap):
            return ap.rearrange("p a b -> p (a b)")

        def scalar_delta(act, group_norm):
            with act.Fori(0, 6) as i:
                for j in range(4):
                    act.wait_ge(lin_read[j], i + READS["b_conv"][j] + 1)
                    act.activation(wide(W(D_CV, 24, SEQ)[:, bass.ds(i * 4 + j, 1)]), gbuf[j % 2][:, 0:SEQ], ACT.Silu)\
                        .then_inc(S("conv_done"), 1)
            with act.Fori(0, 2) as i:
                for j in range(4):
                    act.wait_ge(units_done, i * 4 + FIRST["b_z"] + j + 1)
                    act.activation(wide(W(D_Z, 8, SEQ)[:, bass.ds(i * 4 + j, 1)]), lin[:, j, 0:SEQ], ACT.Silu)\
                        .then_inc(lin_read[j], 1)
            act.wait_ge(S("ba_full"), 1)
            act.activation(beta, view(pair[0][:, 0, 0:32], (2, 16))[:, :, 0:8], ACT.Sigmoid).then_inc(S("beta_ready"), 1)
            act.wait_ge(S("alpha_ready"), 1)
            act.activation(soft, minus_abs, ACT.Exp).then_inc(S("soft_step"), 1)
            act.wait_ge(S("soft_step"), 1)
            act.activation(soft, soft, ACT.Ln, bias=ones[:, 0:1])
            act.activation(decay_rate, P_("a_log"), ACT.Exp).then_inc(S("soft_ready"), 1)
            act.wait_ge(S("conv_done"), 26)
            group_norm("delta")
            act.wait_ge(S("cum_ready"), 1)
            act.activation(tail, tail, ACT.Exp)
            act.activation(grown, cum[:, 1], ACT.Exp).then_inc(S("grown_ready"), 1)
            for bt in range(4):
                act.wait_ge(S("rows_read"), bt + 1)
                d, dt = W(D_TMP + 1024 * (bt % 2), 4, P), W(D_TMP + 1024 * (bt % 2) + 512, 4, P)
                for pr in range(4):
                    h, n = 2 * bt + pr // 2, pr % 2
                    act.activation(d[:, pr], d[:, pr], ACT.Exp, scale=-1.0, bias=cum[:, n, h:h + 1])
                    act.activation(dt[:, pr], dt[:, pr], ACT.Exp, bias=minus_cum[:, n, h:h + 1])
                act.activation(gbuf[bt % 2][:, 0:SEQ], gbuf[bt % 2][:, 0:SEQ], ACT.Exp).then_inc(S("decay_ready"), 1)
            for m in range(4 * LEVELS):
                act.wait_ge(S("q1_full"), m + 1)
                if m >= 2:
                    act.wait_ge(S("update_full"), m - 1)
                act.activation(W(D_Q1, 2, 512)[:, m % 2], lin[:, m % 2], ACT.Copy).then_inc(S("q1_read"), 1)
            act.wait_ge(S("delta_o_read"), 4)
            group_norm("delta_out")

        def vector_delta(dve, own, link, parts, begin, through, split, group_norm):
            def conv_turn(i, j):
                if isinstance(i, int):
                    t = 4 * i + j
                    w = view(P_("conv_w"), (24, 4))[:, t]
                else:
                    w = wide(view(P_("conv_w"), (24, 4))[:, bass.ds(i * 4 + j, 1)])
                y = gbuf[j % 2]
                dve.wait_ge(units_done, i * 4 + FIRST["b_conv"] + j + 1)
                dve.wait_ge(S("conv_done"), i * 4 + j + 1)
                link(dve.tensor_scalar(y[:, 0:SEQ], lin[:, j, 0:SEQ], w[:, 3:4], None, ALU.mult))
                for back in (1, 2, 3):
                    ins = dve.scalar_tensor_tensor(y[:, back:SEQ], lin[:, j, 0:SEQ - back], w[:, 3 - back:4 - back],
                                                   y[:, back:SEQ], ALU.mult, ALU.add)
                    if back < 3:
                        link(ins)
                ins.then_inc(lin_read[j], 1)
            dve.sem_inc(S("conv_done"), 2)
            through("b_conv", conv_turn)
            begin("b_z")
            through("b_z")
            dve.wait_ge(S("beta_ready"), 1)
            ba = view(pair[0][:, 0, 0:32], (2, 16))
            link(dve.tensor_tensor(alpha, ba[:, :, 8:16], P_("dt_bias").unsqueeze(1).broadcast_to([P, 2, 8]), ALU.add))
            dve.scalar_tensor_tensor(minus_abs, alpha, -1.0, alpha, ALU.mult, ALU.min).then_inc(S("alpha_ready"), 1)
            dve.wait_ge(S("soft_ready"), 1)
            link(dve.scalar_tensor_tensor(soft, alpha, 0.0, soft, ALU.max, ALU.add))
            dve.scalar_tensor_tensor(gate, soft, -1.0, decay_rate.unsqueeze(1).broadcast_to([P, 2, 8]), ALU.mult, ALU.mult)\
                .then_inc(S("gate_ready"), 1)
            group_norm("delta")
            dve.wait_ge(S("cum_full"), 1)
            link(dve.tensor_copy(cum, view(pair[0][:, 1, 0:16], (2, 8))))
            dve.tensor_scalar(minus_cum, cum, -1.0, None, ALU.mult)
            dve.tensor_tensor(tail, pair[0][:, 1, 16:24], cum[:, 0], ALU.subtract).then_inc(S("cum_ready"), 1)
            dve.wait_ge(S("grown_ready"), 1)
            link(dve.scalar_tensor_tensor(minus_grown, grown, -1.0, beta[:, 1], ALU.mult, ALU.mult))
            for r in range(6):
                dve.wait_ge(S("turn_full"), r + 1)
                for c in range(4):
                    h, n = (2 * r + c // 2, c % 2) if r < 4 else (4 * (r - 4) + c, 0)
                    dst = v_rows[:, h, n * P:(n + 1) * P] if r < 4 else k_tail[:, h]
                    by = beta[:, n, h:h + 1] if r < 4 else tail[:, h:h + 1]
                    ins = dve.tensor_scalar(dst, pair[1][:, 1, c * P:(c + 1) * P], by, None, ALU.mult)
                ins.then_inc(S("turn_read"), 1)
            dve.wait_ge(S("delta_tables_in"), 16)
            four = lambda ap: ap.unsqueeze(1).broadcast_to([P, 4, P])
            for bt in range(4):
                d, dt = W(D_TMP + 1024 * (bt % 2), 4, P), W(D_TMP + 1024 * (bt % 2) + 512, 4, P)
                rows = view(pair[0][:, 0], (4, P))
                dve.wait_ge(S("rows_full"), bt + 1)
                dve.tensor_tensor(d, rows, four(delta_table(1)), ALU.add)
                dve.tensor_tensor(dt, rows, four(delta_table(2)), ALU.add)
                dve.tensor_copy(view(gbuf[bt % 2][:, 0:SEQ], (2, P)), view(pair[0][:, 0], (2, 2, P))[:, :, 1]).then_inc(S("rows_read"), 1)
                dve.wait_ge(S("decay_ready"), bt + 1)
                dve.wait_ge(S("products_full"), bt + 1)
                for pr in range(4):
                    h, n = 2 * bt + pr // 2, pr % 2
                    dve.scalar_tensor_tensor(lower[:, 4 * bt + pr], view(pair[0][:, 1], (4, P))[:, pr],
                                             beta[:, n, h:h + 1], d[:, pr], ALU.mult, ALU.mult)
                dve.tensor_tensor(attn_t[:, 4 * bt:4 * bt + 4], view(pair[1][:, 0], (4, P)), dt, ALU.mult)
                q = W(D_CV, 24, SEQ)[:, 2 * bt:2 * bt + 2, P:SEQ]
                dve.tensor_tensor(q, q, view(gbuf[bt % 2][:, 0:SEQ], (2, P)), ALU.mult).then_inc(S("products_read"), 1)
            dve.tensor_copy(inv, ident.unsqueeze(1).broadcast_to([P, 16, P]))
            dve.wait_ge(S("products_read"), 4)
            link(dve.tensor_copy(inv_t, ident.unsqueeze(1).broadcast_to([P, 16, P])))
            for t in range(4 * LEVELS + 1):
                if t < 4 * LEVELS:
                    level, bt = divmod(t, 4)
                    if t >= 2:
                        dve.wait_ge(S("q1_full"), t - 1)
                    dve.tensor_tensor(W(D_TMP + 512 * (t % 2), 4, P), lower[:, 4 * bt:4 * bt + 4],
                                      four(delta_table(3 + level)), ALU.mult).then_inc(S("level_ready"), 1)
                if t:
                    m = t - 1
                    level, bt = divmod(m, 4)
                    c = slice(4 * bt, 4 * bt + 4)
                    dve.wait_ge(S("update_full"), m + 1)
                    ins = dve.tensor_tensor(inv_t[:, c], inv_t[:, c], view(lin[:, 2 + m % 2], (4, P)), ALU.subtract)
                    if level < LEVELS - 1:
                        ins = dve.tensor_tensor(inv[:, c], inv[:, c], view(pair[m % 2][:, 0], (4, P)), ALU.subtract)
                    ins.then_inc(S("update_done"), 1)
            for q in range(8):
                step, hb = divmod(q, 2)
                dve.wait_ge(S("scan_full"), q + 1)
                src = view(lin[:, 2 * (step % 2) + hb], (4, P))
                hs = slice(4 * hb, 4 * hb + 4)
                by_head = lambda n: new_v.rearrange("p (h n) e -> p h n e", n=2)[:, hs, n]
                if step == 0:
                    ins = dve.tensor_copy(by_head(0), src)
                if step == 1:
                    ins = dve.tensor_copy(state[:, hs], src)
                if step == 2:
                    for h in range(4 * hb, 4 * hb + 4):
                        ins = dve.scalar_tensor_tensor(mixed[:, h], src[:, h - 4 * hb], minus_grown[:, h:h + 1],
                                                       v_rows[:, h, P:SEQ], ALU.mult, ALU.add)
                if step == 3:
                    ins = dve.tensor_copy(by_head(1), src)
                ins.then_inc(S("scan_read"), 1)
            o = W(D_CV + 4096, 4, 512)
            for n in range(4):
                dve.wait_ge(S("delta_o_full"), n + 1)
                dve.tensor_copy(o[:, n], pair[n % 2][:, n // 2]).then_inc(S("delta_o_read"), 1)
            group_norm("delta_out")
            dve.wait_ge(S("group_done"), 2 + 12 + 8 + 4)
            link(dve.tensor_tensor(W(D_Z, 2048), W(D_Z, 2048), W(D_CV + 4096, 2048), ALU.mult))
            parts(R(OB_HI, 2048), R(OB_LO, 2048), W(D_Z, 2048), S("ob_ready"))

        logits = view(small[:, 256:296], (2, 20))
        combine = view(small[:, 304:336], (2, 16))
        r_exp, r_hot, r_sel, r_one, r_two, r_w = (view(small[:, a:a + 8], (2, 4)) for a in (336, 344, 352, 360, 368, 376))
        r_sc = small[:, 384:404]
        desc = small[:, 0:4]

        def scalar_moe(act):
            act.wait_ge(S("router_step"), 1)
            act.activation(r_exp, r_exp, ACT.Exp).then_inc(S("router_exp"), 1)
            act.wait_ge(S("router_step"), 2)
            act.activation(r_sc[:, 8:10], r_sc[:, 8:10], ACT.Exp).then_inc(S("router_exp"), 1)
            for j in range(8):
                act.wait_ge(S("comb_full"), j + 1)
                act.activation(wide(combine_rows[:, 2 * j:2 * j + 2]), pair[1][:, j % 2], ACT.Copy).then_inc(S("comb_read"), 1)

        def vector_moe(dve, own, link):
            b4 = lambda ap: ap.unsqueeze(2).broadcast_to([P, 2, 4])
            d4 = desc.unsqueeze(1).broadcast_to([P, 2, 4])
            dve.wait_ge(S("logits_full"), 1)
            dve.wait_ge(S("desc_in"), 16)
            link(dve.tensor_tensor(logits, view(pair[0][:, 0, 0:40], (2, 20)),
                                   P_("b_router").unsqueeze(1).broadcast_to([P, 2, 20]), ALU.add))
            gl = logits[:, :, 0:4]
            gmax, gsum, m1, m2, e2, norm_ = (r_sc[:, 2 * n:2 * n + 2] for n in range(6))

            def first_best(dst, src, best, tmp):
                link(dve.tensor_reduce(best, src, AX.X, ALU.max))
                link(dve.tensor_tensor(dst, src, b4(best), ALU.is_equal))
                link(dve.tensor_tensor(dst, dst, d4, ALU.mult))
                link(dve.tensor_reduce(tmp, dst, AX.X, ALU.max))
                link(dve.tensor_tensor(dst, dst, b4(tmp), ALU.is_equal))
            tmp = r_sc[:, 12:14]
            first_best(r_hot, gl, gmax, tmp)
            dve.tensor_tensor(r_exp, gl, b4(gmax), ALU.subtract).then_inc(S("router_step"), 1)
            dve.wait_ge(S("router_exp"), 1)
            link(dve.tensor_reduce(gsum, r_exp, AX.X, ALU.add))
            prod = view(small[:, 404:436], (2, 4, 4))
            el = logits[:, :, 4:20].rearrange("p t (g e) -> p t g e", g=4)
            for tt in range(2):
                ins = dve.tensor_tensor(prod[:, tt], el[:, tt], r_hot[:, tt].unsqueeze(2).broadcast_to([P, 4, 4]), ALU.mult)
            link(ins)
            link(dve.tensor_reduce(r_sel, prod.rearrange("p t g e -> p t e g"), AX.X, ALU.add))
            first_best(r_one, r_sel, m1, tmp)
            link(dve.scalar_tensor_tensor(r_w, r_one, NEG, r_sel, ALU.mult, ALU.add))
            first_best(r_two, r_w, m2, tmp)
            dve.tensor_tensor(e2, m2, m1, ALU.subtract).then_inc(S("router_step"), 1)
            dve.wait_ge(S("router_exp"), 2)
            link(dve.tensor_scalar(norm_, e2, 1.0, None, ALU.add))
            link(dve.tensor_tensor(norm_, norm_, gsum, ALU.mult))
            link(dve.reciprocal(norm_, norm_))
            link(dve.tensor_tensor(r_w, r_two, b4(e2), ALU.mult))
            link(dve.tensor_tensor(r_w, r_w, r_one, ALU.add))
            link(dve.tensor_tensor(r_w, r_w, b4(norm_), ALU.mult))
            for tt in range(2):
                ins = dve.tensor_tensor(combine[:, tt].rearrange("p (g e) -> p g e", g=4),
                                        r_hot[:, tt].unsqueeze(2).broadcast_to([P, 4, 4]),
                                        r_w[:, tt].unsqueeze(1).broadcast_to([P, 4, 4]), ALU.mult)
            ins.then_inc(S("combine_ready"), 1)
            dve.wait_ge(S("comb_read"), 8)

        block = ctx.enter_context(nc.Block())

        def load_unit(sp, stage, i, j):
            bs = body(stage)
            u0 = FIRST[stage] + j
            n = width(stage, j)
            u = i * bs + u0
            if isinstance(i, int) and u < SLOTS:
                pass
            elif FIRST[stage] < SPLIT0 or (isinstance(i, int) and u < SPLIT0 + SLOTS):
                sp.wait_ge(units_done, u - SLOTS + 1)
            else:
                sp.wait_ge(weights_split, u - SLOTS + 1 - SPLIT0)
            src = dram["w_" + stage][bass.ds(i * bs + j, 1)].rearrange("a p n -> p (a n)")[:, 0:n]
            sp.dma_start(raw[u0 % SLOTS][:, 0:n], src).then_inc(raw_loaded[u0 % SLOTS], 16)

        def load_stage(sp, stage):
            bs = body(stage)
            whole, rest = divmod(COUNT[stage], bs)
            first = 0
            if stage in ("ada", "up0"):
                for j in range(bs):
                    load_unit(sp, stage, 0, j)
                first = 1
            if whole - first >= 2:
                with sp.Fori(first, whole) as i:
                    for j in range(bs):
                        load_unit(sp, stage, i, j)
            else:
                for i in range(first, whole):
                    for j in range(bs):
                        load_unit(sp, stage, i, j)
            for j in range(rest):
                load_unit(sp, stage, whole, j)

        INNER = {"up0": 0, "up1": FF_TILES, "up2": 2 * FF_TILES, "up3": 3 * FF_TILES, "exp_up": 4 * FF_TILES}

        PHASE_STAGES = {
            "ada": ["ada"], "ffn0": ["up0", "down0"], "mixer_a": ["ab_uqk", "ab_v", "ab_out"],
            "ffn1": ["up1", "down1"], "ffn2": ["up2", "down2"],
            "mla": ["mla_in", "mla_uq", "mla_uk", "mla_uv", "mla_o"], "ffn3": ["up3", "down3"], "final": [],
            "attn_b": ["b_qk", "b_v"], "delta": ["b_conv", "b_z", ], "merge": ["b_gates", "branch_a", "branch_b", "b_out"],
            "moe": ["exp_up", "exp_down"], "ple": ["ple_gate", "ple_w"],
        }

        @block.sync
        def _(sp):
            for name, dst in (("params", par[:, :]), ("c_base", base[:, :])):
                sp.dma_start(dst, dram[name]).then_inc(S("params_in"), 16)
            sp.dma_start(x[:, :, :], dram["x_t"]).then_inc(S("x_in"), 16)
            for ph in phases:
                for stage in PHASE_STAGES[ph]:
                    load_stage(sp, stage)

        @block.gpsimd
        def _(pool):
            if "mixer_a" in phases:
                pool.wait_ge(lin_read[3], READS["down0 end"][3])
                pool.dma_start(W(A_DFT, 1280), dram["c_dft"]).then_inc(S("dft_in"), 16)
                pool.dma_start(W(A_BIAS, 4096), dram["bias"].rearrange("p a b c -> p (a b c)")).then_inc(S("bias_in"), 16)
            if "mla" in phases:
                pool.wait_ge(lin_read[3], READS["down2 end"][3])
                pool.dma_start(W(M_ROPE, 640), dram["c_rope"]).then_inc(S("rope_in"), 16)
            if "attn_b" in phases:
                pool.wait_ge(lin_read[3], READS["down3 end"][3])
                pool.dma_start(W(B_BANDS, 1152), dram["c_bands"]).then_inc(S("bands_in"), 16)
                pool.dma_start(W(OA_HI, 288), dram["w_small"]).then_inc(S("w_small_in"), 16)
                pool.wait_ge(S("h_ready"), 2 * 7 + 1)
                pool.dma_start(h_wide[:, 0:5, SEQ:TOK], dram["c_delta"].rearrange("p (a b) -> p a b", a=5))\
                    .then_inc(S("delta_tables_in"), 16)
                pool.dma_start(small[:, 0:4], dram["c_desc"]).then_inc(S("desc_in"), 16)
            if "ple" in phases:
                pool.wait_ge(lin_read[3], READS["exp_down end"][3])
                pool.dma_start(W(20480, QT, SEQ), dram["ple"]).then_inc(S("ple_in"), 16)

        @block.scalar
        def _(act):
            own = Tally(act_own)
            item = [0]
            group = [0]
            squares = [0]

            def done_here(ins):
                act.wait_ge(act_own, own.inc(ins))

            def norm(ph):
                n, cols, src = NORMS[ph]
                for k in range(KT):
                    if src == "load":
                        if k == 0:
                            act.wait_ge(S("x_in"), 16)
                    elif src == "final":
                        if k % 4 == 0:
                            act.wait_ge(S("h_ready"), 2 * 6 + k // 4 + 1)
                    else:
                        act.wait_ge(lin_read[k % 4], READS[src][k % 4] + k // 4 + 1)
                    act.activation(squares_of(ph)[:, k, 0:cols], x[:, k, 0:cols], ACT.Square).then_inc(S("sq_ready"), 1)
                act.wait_ge(S("sums_done"), n + 1)
                act.activation(std[0][:, 0:cols], norm_bank[:, 0:cols], ACT.Sqrt, scale=1 / D, bias=eps[:, :])\
                    .then_inc(S("std_ready"), 1)
                if n < 6:
                    layer, m = n // 3, (0, 3, 6)[n % 3]
                    for k in range(KT):
                        if k % 4 == 0:
                            act.wait_ge(S("h_scaled"), 2 * n + k // 4 + 1)
                        for s in range(cols // SEQ):
                            v = W(0, KT, TOK)[:, k, s * SEQ:(s + 1) * SEQ]
                            ins = act.activation(v, v, ACT.Identity, bias=mod(layer, m, k, s))
                        if k % 4 == 3:
                            ins.then_inc(S("h_shifted"), 1)

            def copy_out(stage, cols, place, func=ACT.Copy, scale=1.0, wait=None):
                def one(i, j):
                    b = j % 4
                    act.wait_ge(units_done, i * 4 + FIRST[stage] + j + 1)
                    act.activation(place(i * 4 + j), lin[:, b, 0:cols], func, scale=scale).then_inc(lin_read[b], 1)
                n = COUNT[stage] // 4
                if n > 1:
                    with act.Fori(0, n) as i:
                        for j in range(4):
                            one(i, j)
                else:
                    for j in range(4):
                        one(0, j)

            def ffn(stage, cols):
                with act.Fori(0, COUNT[stage] // 4) as i:
                    for j in range(2):
                        g = 2 * j
                        act.wait_ge(units_done, i * 4 + FIRST[stage] + g + 1)
                        act.wait_ge(inner_ready, i * 2 + INNER[stage] + j + 1)
                        act.activation(gbuf[j][:, 0:cols], lin[:, g, 0:cols], ACT.Silu).then_inc(lin_read[g], 1)

            def group_norm(kind):
                items = group_norms(kind)
                buf = {}

                def square(n):
                    for src in items[n][0]:
                        q = squares[0]
                        if q >= 2:
                            act.wait_ge(S("group_summed"), q - 1)
                        act.activation(sqb[q % 2][:, 0:src.shape[1]], src, ACT.Square).then_inc(S("group_sq"), 1)
                        squares[0] += 1

                def root(n):
                    sources, _, inv, _ = items[n]
                    cols = sources[0].shape[1]
                    g = group[0]
                    act.wait_ge(S("group_summed"), buf[n])
                    if g >= 2:
                        act.wait_ge(S("group_done"), g - 1)
                    else:
                        act.wait_ge(S("h_ready"), 2 * NORMS["mla"][0] + 2)
                    act.activation(std[g % 2][:, 0:cols], pair[1][:, g % 2, 0:cols], ACT.Sqrt, scale=inv, bias=eps[:, :])\
                        .then_inc(S("group_std"), 1)
                    group[0] += 1

                for n in range(len(items) + 1):
                    if n < len(items):
                        square(n)
                        buf[n] = squares[0]
                    if n:
                        root(n - 1)

            def softmaxes(kind, p_at, pt_at, p_len):
                items = softmax_items(kind)
                N = len(items)
                for t in range(N + 1):
                    if t < N:
                        _, cols, scale, _, _, _ = items[t]
                        n = item[0] + t
                        act.wait_ge(S("max_ready"), n + 1)
                        if t >= 2:
                            act.wait_ge(S("turned_full"), n - 1)
                        act.activation(W(p_at, 2, p_len)[:, t % 2, 0:cols], pair[t % 2].rearrange("p a b -> p (a b)")[:, 0:cols],
                                       ACT.Exp, bias=small[:, 16 + n % 2:17 + n % 2], scale=scale,
                                       accum_out=small[:, 18 + n % 2:19 + n % 2]).then_inc(S("exp_ready"), 1)
                    if t:
                        n, cols = item[0] + t - 1, items[t - 1][1]
                        act.wait_ge(S("turned_full"), n + 1)
                        if t - 1 >= 2:
                            act.wait_ge(S("o_full"), n - 1)
                        act.activation(W(pt_at, 2, p_len)[:, (t - 1) % 2, 0:cols],
                                       lin.rearrange("p a b -> p (a b)")[:, 0:cols], ACT.Copy)\
                            .then_inc(S("turned_read"), 1)
                item[0] += N

            act.wait_ge(S("params_in"), 32)
            act.activation(cond[:, :, :], view(P_("cond"), (KT, 2)), ACT.Silu).then_inc(S("cond_ready"), 1)
            row = W(0, 2, 512)
            with act.Fori(0, 18) as i:
                for j in range(2):
                    act.wait_ge(units_done, i * 8 + 4 * j + 4)
                    act.wait_ge(S("ada_turned"), i * 2 + j + 1)
                    act.activation(row[0:2, j, :], lin[0:2, j, :], ACT.Copy).then_inc(lin_read[j], 1)

            for ph in phases:
                if ph in NORMS:
                    norm(ph)
                if ph in ("ffn0", "ffn1", "ffn2", "ffn3"):
                    ffn("up" + ph[3], TOK if ph != "ffn3" else SEQ)
                if ph == "mixer_a":
                    copy_out("ab_uqk", TOK, lambda j: W(A_U, 12, TOK)[:, bass.ds(j, 1)].rearrange("p a t -> p (a t)"))
                    for b in range(4):
                        act.wait_ge(units_done, FIRST["ab_v"] + 4)
                        act.activation(W(A_V, 4, 512)[:, b], lin[:, b], ACT.Copy).then_inc(lin_read[b], 1)
                    for n in range(8):
                        act.wait_ge(S("dft_inner"), n + 1)
                        if n >= 2:
                            act.wait_ge(S("dft_outer"), n - 1)
                        act.activation(W(A_FV, 2, 512)[:, n % 2], pair[0][:, n % 2], ACT.Copy).then_inc(S("dft_inner_read"), 1)
                    softmaxes("window", A_P, A_PT, 512)
                    softmaxes("context", A_P, A_PT, 512)
                if ph == "mla":
                    for j in range(5):
                        act.wait_ge(units_done, FIRST["mla_in"] + j + 1)
                        cols = SEQ if j < 3 else TOK
                        dst = W(M_CQ, 3, SEQ)[:, j] if j < 3 else W(M_CKV if j == 3 else M_KR, TOK)
                        act.activation(dst, lin[:, j % 4, 0:cols], ACT.Copy).then_inc(lin_read[j % 4], 1)
                    act.wait_ge(lin_read[0], READS["mla_in end"][0])
                    act.wait_ge(lin_read[3], READS["mla_in end"][3])
                    group_norm("mla")
                    for n in range(12):
                        act.wait_ge(units_done, FIRST["mla_uq"] + n // 2 + 1)
                        dst = W(M_QN, 8, SEQ)[:, n] if n < 8 else W(M_QR, 4, SEQ)[:, n - 8]
                        act.activation(dst, lin[:, n % 4, 0:SEQ], ACT.Copy).then_inc(lin_read[n % 4], 1)
                    for n in range(8):
                        act.wait_ge(units_done, FIRST["mla_uk"] + n // 4 + 1)
                        act.activation(W(M_KN, 8, TOK)[:, n], lin[:, n % 4], ACT.Copy).then_inc(lin_read[n % 4], 1)
                    for n in range(8):
                        act.wait_ge(units_done, FIRST["mla_uv"] + n // 4 + 1)
                        act.activation(W(M_V, 4, 1024)[:, n % 4, (n // 4) * 512:(n // 4 + 1) * 512], lin[:, n % 4],
                                       ACT.Copy).then_inc(lin_read[n % 4], 1)
                    softmaxes("mla", M_P, M_PT, 512)
                if ph == "attn_b":
                    copy_out("b_qk", SEQ, lambda j: W(B_QK, 24, SEQ)[:, bass.ds(j, 1)].rearrange("p a t -> p (a t)"))
                    for nb in range(3):
                        for tt in range(2):
                            b = 2 * (nb % 2) + tt
                            act.wait_ge(units_done, FIRST["b_v"] + 4 * nb + 4)
                            act.activation(W(B_V, QT, 1536)[:, tt, nb * 512:(nb + 1) * 512], lin[:, b], ACT.Copy)\
                                .then_inc(lin_read[b], 1)
                    group_norm("qk")
                    softmaxes("banded", B_P, B_PT, 768)
                if ph == "delta":
                    scalar_delta(act, group_norm)
                if ph == "merge":
                    copy_out("b_gates", SEQ, lambda j: W(C_GATE, 16, SEQ)[:, bass.ds(j, 1)].rearrange("p a t -> p (a t)"),
                             func=ACT.Sigmoid)
                if ph == "moe":
                    scalar_moe(act)
                    ffn("exp_up", SEQ)
                if ph == "ple":
                    copy_out("ple_gate", SEQ, lambda j: (W(8192 + 0, 8, SEQ)[:, j] if isinstance(j, int) else
                                                         W(8192, 8, SEQ)[:, bass.ds(j, 1)].rearrange("p a t -> p (a t)")),
                             func=ACT.Sigmoid)

            act.wait_ge(S("x_final"), 1)
            act.dma_start(out, x[:, :, 0:out.shape[2]]).then_inc(S("out_done"), 16)
            act.wait_ge(S("out_done"), 16)

        @block.vector
        def _(dve):
            own = Tally(vec)
            item, group = [0], [0]

            def link(ins):
                dve.wait_ge(vec, own.inc(ins))

            def split(stage, i, j):
                bs = body(stage)
                j, i = j % bs, i + j // bs
                u0 = FIRST[stage] + j
                u, s, n = i * bs + u0, (FIRST[stage] + j) % SLOTS, width(stage, j)
                dve.wait_ge(raw_loaded[s], (i * (bs // SLOTS) + u0 // SLOTS + 1) * 16)
                dve.wait_ge(units_done, u - SLOTS + 1)
                link(dve.tensor_copy(whi[s][:, 0:n], raw[s][:, 0:n]))
                dve.tensor_tensor(wlo[s][:, 0:n], raw[s][:, 0:n], whi[s][:, 0:n].bitcast(F32), ALU.subtract)\
                    .then_inc(weights_split, 1)

            def begin(stage):
                for j in range(LOOK):
                    split(stage, 0, j)

            def through(stage, turn=None):
                bs, n = body(stage), COUNT[stage]
                whole, rest = divmod(n, bs)

                def one(i, j, last):
                    ahead = j + LOOK
                    if not last or i * bs + ahead < n:
                        split(stage, i, ahead)
                    if turn:
                        turn(i, j)

                loops = whole - 1 if rest == 0 else whole - (1 if rest < LOOK else 0)
                if loops >= 2:
                    with counted(dve, loops, (own, per_turn(stage, turn))) as i:
                        for j in range(bs):
                            one(i, j, False)
                else:
                    loops = 0
                for i in range(loops, whole + (rest > 0)):
                    for j in range(bs if i < whole else rest):
                        one(i, j, True)

            def per_turn(stage, turn):
                return body(stage) + (TURN_STEPS[turn.__name__] if turn else 0)

            TURN_STEPS = {"ffn_turn": 2, "expert_turn": 4, "down_turn": 0, "conv_turn": 12}

            def parts(hi, lo, src, sem_):
                link(dve.tensor_copy(hi, src))
                dve.tensor_tensor(lo, src, hi.bitcast(F32), ALU.subtract).then_inc(sem_, 1)

            def norm(ph):
                n, cols, _ = NORMS[ph]
                dve.wait_ge(S("std_ready"), n + 1)
                link(dve.reciprocal(std[1][:, 0:cols], std[0][:, 0:cols]))
                for half in range(2):
                    for k in range(4 * half, 4 * half + 4):
                        for s in range(cols // SEQ):
                            t = slice(s * SEQ, (s + 1) * SEQ)
                            dst = x[:, k, t] if ph == "final" else W(0, KT, TOK)[:, k, t]
                            ins = dve.scalar_tensor_tensor(dst, x[:, k, t], norm_gain(ph, k, s), std[1][:, t],
                                                           ALU.mult, ALU.mult)
                    if ph == "final":
                        ins.then_inc(S("h_ready"), 1)
                    elif n < 6:
                        ins.then_inc(S("h_scaled"), 1)
                    else:
                        link(ins)
                if ph == "final":
                    return
                for half in range(2):
                    k = slice(4 * half, 4 * half + 4)
                    if n < 6:
                        dve.wait_ge(S("h_shifted"), 2 * n + half + 1)
                    parts(h_hi[:, k, 0:cols], h_lo[:, k, 0:cols], W(0, KT, TOK)[:, k, 0:cols], S("h_ready"))

            def inner(stage, cols, i, j):
                p = j // 2
                t = i * 2 + p
                experts = stage == "exp_up"
                dve.wait_ge(units_done, i * 4 + FIRST[stage] + j + 1)
                dve.wait_ge(lin_read[j - 1], i + READS[stage][j - 1] + 1)
                g = gbuf[p][:, 0:cols]
                if experts:
                    row = combine_rows[:, bass.ds(i, 1), :].rearrange("p a t -> p (a t)") if not isinstance(i, int) \
                        else combine_rows[:, i]
                    link(dve.tensor_tensor(g, g, row, ALU.mult))
                dve.tensor_tensor(g, g, lin[:, j, 0:cols], ALU.mult).then_inc(lin_read[j], 1)
                dve.wait_ge(lin_read[j], i + READS[stage][j] + 1)
                hi, lo = (e_hi, e_lo) if experts else (a_hi, a_lo)
                at = lambda v: (v[:, t, 0:cols] if isinstance(t, int)
                                else v[:, bass.ds(t, 1), 0:cols].rearrange("p a t -> p (a t)"))
                link(dve.tensor_copy(at(hi), g))
                dve.tensor_tensor(at(lo), g, at(hi).bitcast(F32), ALU.subtract).then_inc(inner_ready, 1)

            def ffn_up(stage, cols):
                def ffn_turn(i, j):
                    if j % 2:
                        inner(stage, cols, i, j)

                def expert_turn(i, j):
                    ffn_turn(i, j)

                through(stage, expert_turn if stage == "exp_up" else ffn_turn)

            def add_to_x(stage, j_unit, d, b, nth, scale_of, cols):
                dve.wait_ge(units_done, j_unit + 1)
                for s in range(cols // SEQ):
                    t = slice(s * SEQ, (s + 1) * SEQ)
                    xs = x[:, d, t] if isinstance(d, int) else x[:, bass.ds(d, 1), t].rearrange("p a t -> p (a t)")
                    if scale_of is None:
                        ins = dve.tensor_tensor(xs, lin[:, b, t], xs, ALU.add)
                    else:
                        ins = dve.scalar_tensor_tensor(xs, lin[:, b, t], scale_of(d, s), xs, ALU.mult, ALU.add)
                ins.then_inc(lin_read[b], 1)

            def down(stage, cols, layer=None, m=None):
                per = COUNT[stage] // KT

                def gate(d, s):
                    if isinstance(d, int):
                        return mod(layer, m, d, s)
                    return mods[:, bass.ds(d + (layer * 72 + m * 8), 1), s:s + 1].rearrange("p a b -> p (a b)")

                def down_turn(i, j):
                    if j % per == per - 1:
                        outs = body(stage) // per
                        d = i * outs + j // per
                        b = (j // per) % 4
                        add_to_x(stage, i * body(stage) + FIRST[stage] + j, d, b, None,
                                 gate if layer is not None else None, cols)
                through(stage, down_turn)

            def out_stage(stage, cols, layer=None, m=None):
                for j in range(KT):
                    if j + LOOK < KT:
                        split(stage, (j + LOOK) // 4, (j + LOOK) % 4)
                    add_to_x(stage, FIRST[stage] + j, j, j % 4, None,
                             (lambda d, s: mod(layer, m, d, s)) if layer is not None else None, cols)

            def group_norm(kind):
                for sources, _, _, outs in group_norms(kind):
                    cols = sources[0].shape[1]
                    g = group[0]
                    dve.wait_ge(S("group_std"), g + 1)
                    r = std[g % 2][:, 0:cols]
                    link(dve.reciprocal(r, r))
                    for src, gain, dst in outs:
                        ins = dve.scalar_tensor_tensor(dst, src, gain, r, ALU.mult, ALU.mult)
                    ins.then_inc(S("group_done"), 1)
                    group[0] += 1

            def softmaxes(kind, p_at, p_len):
                items = softmax_items(kind)
                N = len(items)
                for t in range(N + 2):
                    if t < N:
                        _, cols, scale, _, _, _ = items[t]
                        n = item[0] + t
                        dve.wait_ge(S("scores_full"), n + 1)
                        if t >= 2:
                            dve.wait_ge(S("exp_ready"), n - 1)
                        m = small[:, 16 + n % 2:17 + n % 2]
                        link(dve.tensor_reduce(m, pair[t % 2].rearrange("p a b -> p (a b)")[:, 0:cols], AX.X, ALU.max))
                        dve.tensor_scalar(m, m, -scale, None, ALU.mult).then_inc(S("max_ready"), 1)
                    if 1 <= t <= N:
                        n, cols = item[0] + t - 1, items[t - 1][1]
                        dve.wait_ge(S("exp_ready"), n + 1)
                        r = small[:, 20 + n % 2:21 + n % 2]
                        link(dve.reciprocal(r, small[:, 18 + n % 2:19 + n % 2]))
                        p = W(p_at, 2, p_len)[:, (t - 1) % 2, 0:cols]
                        dve.tensor_scalar(p, p, r, None, ALU.mult).then_inc(S("probs_ready"), 1)
                    if t >= 2:
                        n, (_, _, _, _, dst, rows) = item[0] + t - 2, items[t - 2]
                        dve.wait_ge(S("o_full"), n + 1)
                        dve.tensor_copy(dst, lin[rows, 2 + (t - 2) % 2, 0:P]).then_inc(S("o_read"), 1)
                item[0] += N
                dve.wait_ge(S("o_read"), item[0])

            link(dve.memset(eps[:, :], EPS))
            for b in range(4):
                dve.sem_inc(lin_read[b], 1)
            dve.sem_inc(inner_ready, 2)
            dve.sem_inc(S("mods_copied"), 2)

            flat = mods.rearrange("p a b -> p (a b)")
            with dve.Fori(0, 18) as i:
                for j in range(2):
                    dve.wait_ge(S("ada_turned"), i * 2 + j + 3)
                    dve.tensor_copy(flat[:, bass.ds((i * 2 + j) * 8, 8)], pair[0][:, j, 0:8]).then_inc(S("mods_copied"), 1)
            dve.wait_ge(S("mods_copied"), 38)
            dve.wait_ge(S("params_in"), 32)
            link(dve.tensor_tensor(mods[:, :, :], mods[:, :, :], P_("ada_b").unsqueeze(2).broadcast_to([P, 144, 2]), ALU.add))
            for layer in range(2):
                for n, m in enumerate((1, 4, 7)):
                    r = layer * 72 + m * 8
                    g = P_("norm_g")[:, (layer * 3 + n) * 8:(layer * 3 + n) * 8 + 8].unsqueeze(2).broadcast_to([P, 8, 2])
                    link(dve.scalar_tensor_tensor(gains[:, layer * 3 + n], mods[:, r:r + 8, :], 1.0, g, ALU.add, ALU.mult))
                for m in (2, 8):
                    r = layer * 72 + m * 8
                    link(dve.tensor_scalar(mods[:, r:r + 8, :], mods[:, r:r + 8, :], 0.5, None, ALU.mult))

            for ph in phases:
                if ph.startswith("ffn"):
                    n = ph[3]
                    layer, m, cols = int(n) // 2, (2, 8)[int(n) % 2], TOK if ph != "ffn3" else SEQ
                    begin("up" + n)
                    norm(ph)
                    ffn_up("up" + n, cols)
                    begin("down" + n)
                    down("down" + n, cols, layer, m)
                if ph == "mixer_a":
                    begin("ab_uqk")
                    norm(ph)
                    through("ab_uqk")
                    begin("ab_v")
                    through("ab_v")
                    begin("ab_out")
                    for b in range(4):
                        dve.wait_ge(lin_read[b], READS["ab_v end"][b])
                    dve.tensor_scalar(W(A_Q, 2048), W(A_Q, 2048), NA_SCALE, None, ALU.mult).then_inc(S("na_q_ready"), 1)
                    for n in range(8):
                        g, s = n // 2, n % 2
                        dve.wait_ge(S("dft_outer"), n + 1)
                        dve.tensor_copy(W(A_CAT, KT, TOK)[:, g, s * SEQ:(s + 1) * SEQ], pair[1][:, n % 2, 0:SEQ])\
                            .then_inc(S("dft_outer_read"), 1)
                    softmaxes("window", A_P, 512)
                    softmaxes("context", A_P, 512)
                    for half in range(2):
                        k = slice(4 * half, 4 * half + 4)
                        parts(h_hi[:, k, :], h_lo[:, k, :], W(A_CAT, KT, TOK)[:, k, :], S("cat_ready"))
                    out_stage("ab_out", TOK, 0, 5)
                if ph == "mla":
                    begin("mla_in")
                    norm(ph)
                    through("mla_in")
                    begin("mla_uq")
                    group_norm("mla")
                    dve.wait_ge(S("group_done"), 2)
                    parts(R(M_CQH, 768), R(M_CQL, 768), W(M_CQ, 768), S("latents_ready"))
                    parts(R(M_CKH, 512), R(M_CKL, 512), W(M_CKV, 512), S("latents_ready"))
                    through("mla_uq")
                    begin("mla_uk")
                    begin("mla_uv")
                    begin("mla_o")
                    dve.wait_ge(S("rope_in"), 16)
                    rope = W(M_ROPE, 640)
                    cos, sin = rope[:, P:P + SEQ], rope[:, P + SEQ:P + 2 * SEQ]
                    for b in range(4):
                        dve.wait_ge(lin_read[b], READS["mla_uq end"][b])
                    link(dve.tensor_copy(W(M_KRR, TOK)[:, SEQ:TOK], W(M_KR, TOK)[:, SEQ:TOK]))
                    for n in range(5):
                        src = W(M_QR, 4, SEQ)[:, n] if n < 4 else W(M_KR, TOK)[:, 0:SEQ]
                        dst = W(M_QRR, 4, SEQ)[:, n] if n < 4 else W(M_KRR, TOK)[:, 0:SEQ]
                        dve.wait_ge(S("rotated"), n + 1)
                        link(dve.tensor_tensor(dst, pair[0][:, n % 2, 0:SEQ], sin, ALU.mult))
                        dve.tensor_tensor(src, src, cos, ALU.mult).then_inc(S("rotated_read"), 1)
                        dve.wait_ge(S("rotated_read"), n + 1)
                        dve.tensor_tensor(dst, dst, src, ALU.add).then_inc(S("rope_done"), 1)
                    softmaxes("mla", M_P, 512)
                    for half in range(2):
                        k = slice(4 * half, 4 * half + 4)
                        parts(h_hi[:, k, 0:SEQ], h_lo[:, k, 0:SEQ], W(M_O, 8, SEQ)[:, k, :], S("cat_ready"))
                    out_stage("mla_o", SEQ, 1, 5)
                if ph == "final":
                    norm(ph)
                if ph == "attn_b":
                    begin("b_qk")
                    norm(ph)
                    dve.wait_ge(S("w_small_in"), 16)
                    parts(small_hi[:, :], small_lo[:, :], W(OA_HI, 288), S("small_split"))
                    through("b_qk")
                    begin("b_v")
                    through("b_v")
                    begin("b_conv")
                    group_norm("qk")
                    softmaxes("banded", B_P, 768)
                    parts(R(OA_HI, 1024), R(OA_LO, 1024), W(B_OA, 1024), S("oa_ready"))
                if ph == "delta":
                    vector_delta(dve, own, link, parts, begin, through, split, group_norm)
                if ph == "merge":
                    begin("b_gates")
                    through("b_gates")
                    begin("branch_a")
                    for b in range(4):
                        dve.wait_ge(lin_read[b], READS["b_gates end"][b])
                    for n in range(8):
                        if n % 2 == 0 and n // 2 + LOOK < 4:
                            split("branch_a", 0, n // 2 + LOOK)
                        if n == 6:
                            begin("branch_b")
                        dve.wait_ge(units_done, FIRST["branch_a"] + n // 2 + 1)
                        dve.tensor_tensor(W(C_M, 8, SEQ)[:, n], lin[:, n % 4, 0:SEQ], W(C_GATE, 16, SEQ)[:, n], ALU.mult)\
                            .then_inc(lin_read[n % 4], 1)
                    for n in range(8):
                        if n + LOOK < 8:
                            split("branch_b", (n + LOOK) // 4, (n + LOOK) % 4)
                        dve.wait_ge(units_done, FIRST["branch_b"] + n + 1)
                        t = W(C_GATE, 16, SEQ)[:, 8 + n]
                        dve.tensor_tensor(t, lin[:, n % 4, 0:SEQ], t, ALU.mult).then_inc(lin_read[n % 4], 1)
                        dve.wait_ge(lin_read[n % 4], READS["branch_b"][n % 4] + n // 4 + 1)
                        m = W(C_M, 8, SEQ)[:, n]
                        link(dve.tensor_tensor(m, m, t, ALU.add))
                    begin("b_out")
                    parts(R(C_MH, 2048), R(C_ML, 2048), W(C_M, 2048), S("merged_ready"))
                    out_stage("b_out", SEQ)
                if ph == "moe":
                    begin("exp_up")
                    norm(ph)
                    vector_moe(dve, own, link)
                    ffn_up("exp_up", SEQ)
                    begin("exp_down")
                    down("exp_down", SEQ)
                if ph == "ple":
                    begin("ple_gate")
                    norm(ph)
                    dve.wait_ge(S("ple_in"), 16)
                    parts(R(0, 512), R(512, 512), W(20480, 512), S("ple_split"))
                    for j in range(8):
                        if j + LOOK < 8:
                            split("ple_gate", (j + LOOK) // 4, (j + LOOK) % 4)
                    begin("ple_w")
                    for b in range(4):
                        dve.wait_ge(lin_read[b], READS["ple_gate end"][b])
                    for n in range(8):
                        dve.wait_ge(units_done, FIRST["ple_w"] + n // 4 + 1)
                        t = W(8192, 8, SEQ)[:, n]
                        dve.tensor_tensor(t, lin[:, n % 4, 0:SEQ], t, ALU.mult).then_inc(lin_read[n % 4], 1)
                        dve.wait_ge(lin_read[n % 4], READS["ple_w"][n % 4] + n // 4 + 1)
                        link(dve.tensor_tensor(x[:, n, 0:SEQ], x[:, n, 0:SEQ], t, ALU.add))
            link(dve.tensor_copy(small[:, 22:23], eps[:, :]))
            dve.sem_inc(S("x_final"), 1)

        @block.tensor
        def _(pe):
            item, group, squares = [0], [0], [0]

            def ready(stage, i, j):
                pe.wait_ge(weights_split, i * body(stage) + (FIRST[stage] + j - SPLIT0 + 1))
                return (FIRST[stage] + j) % SLOTS

            def bank_free(stage, b, nth):
                pe.wait_ge(lin_read[b], nth + READS[stage][b])

            def stationary(out_, slot, cols, hi, lo, start, stop):
                for n, c in enumerate(cols):
                    a, b = whi[slot][:, c * P:(c + 1) * P], wlo[slot][:, c * P:(c + 1) * P]
                    pe.matmul(out_, a, hi[n], start=start and n == 0, stop=False)
                    pe.matmul(out_, a, lo[n], start=False, stop=False)
                    ins = pe.matmul(out_, b, hi[n], start=False, stop=stop and n == len(cols) - 1)
                return ins

            def streamed(out_, slot, c0, c1, hi, lo, start, stop):
                a, b = whi[slot][:, c0:c1], wlo[slot][:, c0:c1]
                pe.matmul(out_, hi, a, start=start, stop=False)
                pe.matmul(out_, hi, b, start=False, stop=False)
                return pe.matmul(out_, lo, a, start=False, stop=stop)

            def norm(ph):
                n, cols, _ = NORMS[ph]
                for k in range(KT):
                    pe.wait_ge(S("sq_ready"), n * KT + k + 1)
                    ins = pe.matmul(norm_bank[:, 0:cols], ones, squares_of(ph)[:, k, 0:cols], start=k == 0, stop=k == KT - 1)
                ins.then_inc(S("sums_done"), 1)

            def panels(stage, hi, lo):
                def one(i, j):
                    slot = ready(stage, i, j)
                    bank_free(stage, j % 4, i)
                    stationary(lin[:, j % 4, 0:hi[0].shape[1]], slot, range(KT), hi, lo, True, True).then_inc(units_done, 1)
                n, rest = divmod(COUNT[stage], 4)
                if n > 1:
                    with pe.Fori(0, n) as i:
                        for j in range(4):
                            one(i, j)
                else:
                    for i in range(n):
                        for j in range(4):
                            one(i, j)
                return n, rest

            def tiles(v, cols):
                return [v[:, k, 0:cols] for k in range(KT)]

            def ffn(up, down_, cols):
                pe.wait_ge(S("h_ready"), H_READY[up])
                panels(up, tiles(h_hi, cols), tiles(h_lo, cols))
                hi, lo = (e_hi, e_lo) if up == "exp_up" else (a_hi, a_lo)
                total = EXP_TILES if up == "exp_up" else FF_TILES
                per = COUNT[down_] // KT
                with pe.Fori(0, 2) as i:
                    for d in range(4):
                        bank_free(down_, d, i)
                        for j in range(per):
                            slot = ready(down_, i, d * per + j)
                            ks = list(range(8 * j, min(total, 8 * j + 8)))
                            if d == 0:
                                pe.wait_ge(inner_ready, INNER[up] + ks[-1] + 1 + 2)
                            stationary(lin[:, d, 0:cols], slot, range(len(ks)), [hi[:, k, 0:cols] for k in ks],
                                       [lo[:, k, 0:cols] for k in ks], j == 0, j == per - 1).then_inc(units_done, 1)

            H_READY = {"up0": 2, "up1": 6, "up2": 8, "up3": 12, "exp_up": 18}

            def group_norm(kind):
                items = group_norms(kind)
                for sources, mat, _, _ in items:
                    g = group[0]
                    cols = sources[0].shape[1]
                    if g >= 2:
                        pe.wait_ge(S("group_std"), g - 1)
                    for n, src in enumerate(sources):
                        q = squares[0]
                        pe.wait_ge(S("group_sq"), q + 1)
                        pe.matmul(pair[1][:, g % 2, 0:cols], mat, sqb[q % 2][:, 0:cols], start=n == 0,
                                  stop=n == len(sources) - 1).then_inc(S("group_summed"), 1)
                        squares[0] += 1
                    group[0] += 1

            def softmaxes(kind, p_at, pt_at, p_len):
                items = softmax_items(kind)
                N = len(items)
                for t in range(N + 2):
                    if t < N:
                        ops, cols, _, _, _, _ = items[t]
                        n = item[0] + t
                        if t >= 2:
                            pe.wait_ge(S("exp_ready"), n - 1)
                        bank = pair[t % 2].rearrange("p a b -> p (a b)")
                        seen = set()
                        for q, (a, b, lhs, rhs) in enumerate(ops):
                            new = a // 512 not in seen
                            seen.add(a // 512)
                            last = all(o[0] // 512 != a // 512 for o in ops[q + 1:])
                            ins = pe.matmul(bank[:, a:b], lhs, rhs, start=new, stop=last)
                        ins.then_inc(S("scores_full"), 1)
                    if 1 <= t <= N:
                        n, cols = item[0] + t - 1, items[t - 1][1]
                        pe.wait_ge(S("probs_ready"), n + 1)
                        if t >= 2:
                            pe.wait_ge(S("turned_read"), n)
                        for kt in range(cols // P):
                            ins = pe.transpose(lin.rearrange("p a b -> p (a b)")[:, kt * P:(kt + 1) * P],
                                               W(p_at, 2, p_len)[:, (t - 1) % 2, kt * P:(kt + 1) * P], ident)
                        ins.then_inc(S("turned_full"), 1)
                    if t >= 2:
                        n, (_, _, _, values, _, rows) = item[0] + t - 2, items[t - 2]
                        pe.wait_ge(S("turned_read"), n + 1)
                        if t >= 4:
                            pe.wait_ge(S("o_read"), n - 1)
                        turned = W(pt_at, 2, p_len)[:, (t - 2) % 2]
                        for kt, v in enumerate(values):
                            ins = pe.matmul(lin[rows, 2 + (t - 2) % 2, 0:P], v, turned[:, kt * P:(kt + 1) * P],
                                            start=kt == 0, stop=kt == len(values) - 1)
                        ins.then_inc(S("o_full"), 1)
                item[0] += N

            def small_product(bank, c0, width_, sem_):
                for tt in range(QT):
                    t = slice(tt * P, (tt + 1) * P)
                    for k in range(KT):
                        c = slice(c0 + k * width_, c0 + (k + 1) * width_)
                        o = bank[:, tt * width_:(tt + 1) * width_]
                        pe.matmul(o, h_hi[:, k, t], small_hi[:, c], start=k == 0, stop=False)
                        pe.matmul(o, h_hi[:, k, t], small_lo[:, c], start=False, stop=False)
                        ins = pe.matmul(o, h_lo[:, k, t], small_hi[:, c], start=False, stop=k == KT - 1)
                ins.then_inc(sem_, 1)

            pe.sem_inc(S("ada_turned"), 2)
            pe.wait_ge(S("cond_ready"), 1)
            pe.wait_ge(S("params_in"), 32)
            row = W(0, 2, 512)
            with pe.Fori(0, 18) as i:
                for j in range(2):
                    bank_free("ada", j, i)
                    for q in range(4):
                        u = 4 * j + q
                        pe.wait_ge(raw_loaded[q], (i * 2 + j + 1) * 16)
                        for kk in range(2):
                            ins = pe.matmul(lin[0:2, j, :], cond[:, 2 * q + kk, :], raw[q][:, kk * 512:(kk + 1) * 512],
                                            start=q + kk == 0, stop=q + kk == 4)
                        ins.then_inc(units_done, 1)
                for j in range(2):
                    pe.wait_ge(lin_read[j], i + READS["ada"][j] + 1)
                    pe.wait_ge(S("mods_copied"), i * 2 + j + 1)
                    pe.matmul(pair[0][:, j, 0:2], row[0:2, j, 0:P], ident[0:2, 0:2], start=True, stop=True)
                    for c in range(1, 4):
                        ins = pe.transpose(pair[0][:, j, 2 * c:2 * c + 2], row[0:2, j, c * P:(c + 1) * P], ident[0:2, 0:2])
                    ins.then_inc(S("ada_turned"), 1)

            for ph in phases:
                if ph in NORMS:
                    norm(ph)
                if ph.startswith("ffn"):
                    n = ph[3]
                    ffn("up" + n, "down" + n, SEQ if n == "3" else TOK)
                if ph == "mixer_a":
                    pe.wait_ge(S("h_ready"), 4)
                    panels("ab_uqk", tiles(h_hi, TOK), tiles(h_lo, TOK))
                    for j in range(4):
                        slot = ready("ab_v", 0, j)
                        for tt in range(4):
                            if j == 0:
                                bank_free("ab_v", tt, 0)
                            for kk in range(2):
                                k = 2 * j + kk
                                t = slice(tt * P, (tt + 1) * P)
                                ins = streamed(lin[:, tt], slot, kk * 512, kk * 512 + 512, h_hi[:, k, t], h_lo[:, k, t],
                                               k == 0, k == KT - 1)
                        ins.then_inc(units_done, 1)
                    for b in range(4):
                        pe.wait_ge(lin_read[b], READS["ab_v end"][b])
                    pe.wait_ge(S("dft_in"), 16)
                    dft = W(A_DFT, 1280)
                    cos_n, sin_n = view(dft[:, 256:768], (2, SEQ)), view(dft[:, 768:1280], (2, SEQ))
                    for t in range(9):
                        if t < 8:
                            g, s = t // 2, t % 2
                            if t >= 2:
                                pe.wait_ge(S("dft_inner_read"), t - 1)
                            for nt in range(2):
                                q0 = s * SEQ + nt * P
                                ins = pe.matmul(pair[0][:, t % 2, nt * SEQ:(nt + 1) * SEQ], W(A_U, 4, TOK)[:, g, q0:q0 + P],
                                                dft[:, 0:SEQ], start=True, stop=True)
                            ins.then_inc(S("dft_inner"), 1)
                        if t:
                            m = t - 1
                            pe.wait_ge(S("dft_inner_read"), m + 1)
                            if m >= 2:
                                pe.wait_ge(S("dft_outer_read"), m - 1)
                            fv = W(A_FV, 2, 512)[:, m % 2]
                            for nt in range(2):
                                pe.matmul(pair[1][:, m % 2, 0:SEQ], fv[:, nt * SEQ:nt * SEQ + P], cos_n[:, nt], start=nt == 0, stop=False)
                                ins = pe.matmul(pair[1][:, m % 2, 0:SEQ], fv[:, nt * SEQ + P:(nt + 1) * SEQ], sin_n[:, nt],
                                                start=False, stop=nt == 1)
                            ins.then_inc(S("dft_outer"), 1)
                    pe.wait_ge(S("bias_in"), 16)
                    pe.wait_ge(S("na_q_ready"), 1)
                    pe.wait_ge(S("dft_outer_read"), 8)
                    softmaxes("window", A_P, A_PT, 512)
                    softmaxes("context", A_P, A_PT, 512)
                    pe.wait_ge(S("cat_ready"), 2)
                    panels("ab_out", tiles(h_hi, TOK), tiles(h_lo, TOK))
                if ph == "mla":
                    pe.wait_ge(S("h_ready"), 10)
                    for j in range(5):
                        cols = SEQ if j < 3 else TOK
                        slot = ready("mla_in", 0, j)
                        bank_free("mla_in", j % 4, j // 4)
                        stationary(lin[:, j % 4, 0:cols], slot, range(KT), tiles(h_hi, cols), tiles(h_lo, cols), True, True)\
                            .then_inc(units_done, 1)
                    group_norm("mla")
                    pe.wait_ge(S("latents_ready"), 2)
                    cq = [[R(at, 3, SEQ)[:, k] for k in range(3)] for at in (M_CQH, M_CQL)]
                    for j in range(6):
                        slot = ready("mla_uq", 0, j)
                        for half in range(2):
                            n = 2 * j + half
                            bank_free("mla_uq", n % 4, n // 4)
                            ins = stationary(lin[:, n % 4, 0:SEQ], slot, range(3 * half, 3 * half + 3), cq[0], cq[1], True, True)
                        ins.then_inc(units_done, 1)
                    ck = [R(at, TOK) for at in (M_CKH, M_CKL)]
                    for n in range(8):
                        if n % 4 == 0:
                            slot = ready("mla_uk", 0, n // 4)
                        bank_free("mla_uk", n % 4, n // 4)
                        ins = stationary(lin[:, n % 4], slot, [n % 4], [ck[0]], [ck[1]], True, True)
                        if n % 4 == 3:
                            ins.then_inc(units_done, 1)
                    for n in range(8):
                        if n % 4 == 0:
                            slot = ready("mla_uv", 0, n // 4)
                        bank_free("mla_uv", n % 4, n // 4)
                        t = slice((n % 4) * P, (n % 4 + 1) * P)
                        ins = streamed(lin[:, n % 4], slot, 0, 512, ck[0][:, t], ck[1][:, t], True, True)
                        if n % 4 == 3:
                            ins.then_inc(units_done, 1)
                    pe.wait_ge(S("rope_in"), 16)
                    for b in range(4):
                        pe.wait_ge(lin_read[b], READS["mla_uv end"][b])
                    for n in range(5):
                        src = W(M_QR, 4, SEQ)[:, n] if n < 4 else W(M_KR, TOK)[:, 0:SEQ]
                        if n >= 2:
                            pe.wait_ge(S("rotated_read"), n - 1)
                        pe.matmul(pair[0][:, n % 2, 0:SEQ], W(M_ROPE, 640)[:, 0:P], src, start=True, stop=True)\
                            .then_inc(S("rotated"), 1)
                    pe.wait_ge(S("rope_done"), 5)
                    softmaxes("mla", M_P, M_PT, 512)
                    pe.wait_ge(S("cat_ready"), 4)
                    panels("mla_o", tiles(h_hi, SEQ), tiles(h_lo, SEQ))
                if ph == "attn_b":
                    pe.wait_ge(S("h_ready"), 16)
                    panels("b_qk", tiles(h_hi, SEQ), tiles(h_lo, SEQ))
                    for nb in range(3):
                        for j in range(4):
                            slot = ready("b_v", 0, 4 * nb + j)
                            for tt in range(QT):
                                b = 2 * (nb % 2) + tt
                                if j == 0:
                                    bank_free("b_v", b, nb // 2)
                                for kk in range(2):
                                    k = 2 * j + kk
                                    t = slice(tt * P, (tt + 1) * P)
                                    ins = streamed(lin[:, b], slot, kk * 512, kk * 512 + 512, h_hi[:, k, t], h_lo[:, k, t],
                                                   k == 0, k == KT - 1)
                            ins.then_inc(units_done, 1)
                    group_norm("qk")
                    pe.wait_ge(S("group_done"), 14)
                    pe.wait_ge(S("bands_in"), 16)
                    for b in range(4):
                        pe.wait_ge(lin_read[b], READS["b_v end"][b])
                    softmaxes("banded", B_P, B_PT, 768)
                if ph == "delta":
                    pe.wait_ge(S("oa_ready"), 1)
                    panels("b_conv", tiles(h_hi, SEQ), tiles(h_lo, SEQ))
                    panels("b_z", tiles(h_hi, SEQ), tiles(h_lo, SEQ))
                    pe.wait_ge(S("small_split"), 1)
                    small_product(pair[0][:, 0], 0, 16, S("ba_full"))
                    group_norm("delta")
                    pe.wait_ge(S("gate_ready"), 1)
                    pe.wait_ge(S("delta_tables_in"), 16)
                    utri = delta_table(0)
                    pe.matmul(pair[0][:, 1, 0:16], utri, wide(gate), start=True, stop=True)
                    pe.matmul(pair[0][:, 1, 16:24], ones, gate[:, 0], start=True, stop=True).then_inc(S("cum_full"), 1)
                    pe.wait_ge(S("group_done"), 22)
                    q, k, v = (W(D_CV + 2048 * n, 8, SEQ) for n in range(3))
                    for r in range(6):
                        if r:
                            pe.wait_ge(S("turn_read"), r)
                        for c in range(4):
                            h, n = (2 * r + c // 2, c % 2) if r < 4 else (4 * (r - 4) + c, 0)
                            ins = pe.transpose(pair[1][:, 1, c * P:(c + 1) * P], (v if r < 4 else k)[:, h, n * P:(n + 1) * P], ident)
                        ins.then_inc(S("turn_full"), 1)
                    for bt in range(4):
                        if bt:
                            pe.wait_ge(S("rows_read"), bt)
                        else:
                            pe.wait_ge(S("cum_ready"), 1)
                        for pr in range(4):
                            h, n = 2 * bt + pr // 2, pr % 2
                            ins = pe.matmul(pair[0][:, 0, pr * P:(pr + 1) * P], gate[:, n, h:h + 1].to_broadcast([P, P]), utri,
                                            start=True, stop=True)
                        ins.then_inc(S("rows_full"), 1)
                        if bt:
                            pe.wait_ge(S("products_read"), bt)
                        for pr in range(4):
                            h, n = 2 * bt + pr // 2, pr % 2
                            t = slice(n * P, (n + 1) * P)
                            pe.matmul(pair[0][:, 1, pr * P:(pr + 1) * P], k[:, h, t], k[:, h, t], start=True, stop=True)
                            ins = pe.matmul(pair[1][:, 0, pr * P:(pr + 1) * P], k[:, h, t], q[:, h, t], start=True, stop=True)
                        ins.then_inc(S("products_full"), 1)
                    for t in range(4 * LEVELS + 1):
                        if t < 4 * LEVELS:
                            level, bt = divmod(t, 4)
                            pe.wait_ge(S("level_ready"), t + 1)
                            if t >= 4:
                                pe.wait_ge(S("update_done"), t - 3)
                            if t >= 2:
                                pe.wait_ge(S("q1_read"), t - 1)
                            for pr in range(4):
                                ins = pe.matmul(lin[:, t % 2, pr * P:(pr + 1) * P], W(D_TMP + 512 * (t % 2), 4, P)[:, pr],
                                                inv_t[:, 4 * bt + pr], start=True, stop=True)
                            ins.then_inc(S("q1_full"), 1)
                        if t:
                            m = t - 1
                            level, bt = divmod(m, 4)
                            pe.wait_ge(S("q1_read"), m + 1)
                            if m >= 2:
                                pe.wait_ge(S("update_done"), m - 1)
                            for pr in range(4):
                                q1 = W(D_Q1, 2, 4, P)[:, m % 2, pr]
                                ins = pe.matmul(lin[:, 2 + m % 2, pr * P:(pr + 1) * P], inv[:, 4 * bt + pr], q1, start=True, stop=True)
                                if level < LEVELS - 1:
                                    ins = pe.matmul(pair[m % 2][:, 0, pr * P:(pr + 1) * P], q1, inv[:, 4 * bt + pr],
                                                    start=True, stop=True)
                            ins.then_inc(S("update_full"), 1)
                    pe.wait_ge(S("update_done"), 4 * LEVELS)
                    for s_ in range(8):
                        step, hb = divmod(s_, 2)
                        if step:
                            pe.wait_ge(S("scan_read"), s_ - 1)
                        for c in range(4):
                            h = 4 * hb + c
                            lhs, rhs = [(inv_t[:, 2 * h], v_rows[:, h, 0:P]), (k_tail[:, h], new_v[:, 2 * h]),
                                        (k[:, h, P:SEQ], state[:, h]), (inv_t[:, 2 * h + 1], mixed[:, h])][step]
                            ins = pe.matmul(lin[:, 2 * (step % 2) + hb, c * P:(c + 1) * P], lhs, rhs, start=True, stop=True)
                        ins.then_inc(S("scan_full"), 1)
                    pe.wait_ge(S("scan_read"), 8)
                    for n in range(4):
                        for h in (2 * n, 2 * n + 1):
                            o = pair[n % 2][:, n // 2, (h % 2) * SEQ:(h % 2 + 1) * SEQ]
                            pe.matmul(o[:, 0:P], new_v[:, 2 * h], attn_t[:, 2 * h], start=True, stop=True)
                            pe.matmul(o[:, P:SEQ], state[:, h], q[:, h, P:SEQ], start=True, stop=False)
                            ins = pe.matmul(o[:, P:SEQ], new_v[:, 2 * h + 1], attn_t[:, 2 * h + 1], start=False, stop=True)
                        ins.then_inc(S("delta_o_full"), 1)
                    pe.wait_ge(S("delta_o_read"), 4)
                    group_norm("delta_out")
                if ph == "merge":
                    panels("b_gates", tiles(h_hi, SEQ), tiles(h_lo, SEQ))
                    for n in range(8):
                        if n % 2 == 0:
                            slot = ready("branch_a", 0, n // 2)
                        bank_free("branch_a", n % 4, n // 4)
                        oa = [[R(at, 4, SEQ)[:, k] for k in range(4)] for at in (OA_HI, OA_LO)]
                        ins = stationary(lin[:, n % 4, 0:SEQ], slot, range(4 * (n % 2), 4 * (n % 2) + 4), oa[0], oa[1], True, True)
                        if n % 2:
                            ins.then_inc(units_done, 1)
                    pe.wait_ge(S("ob_ready"), 1)
                    panels("branch_b", tiles(R(OB_HI, 8, SEQ), SEQ), tiles(R(OB_LO, 8, SEQ), SEQ))
                    pe.wait_ge(S("merged_ready"), 1)
                    panels("b_out", tiles(R(C_MH, 8, SEQ), SEQ), tiles(R(C_ML, 8, SEQ), SEQ))
                if ph == "moe":
                    pe.wait_ge(S("h_ready"), 18)
                    small_product(pair[0][:, 0], 8 * 16, 20, S("logits_full"))
                    pe.wait_ge(S("combine_ready"), 1)
                    for j in range(8):
                        if j >= 2:
                            pe.wait_ge(S("comb_read"), j - 1)
                        for e in (2 * j, 2 * j + 1):
                            for tt in range(QT):
                                at = (e % 2) * SEQ + tt * P
                                ins = pe.matmul(pair[1][:, j % 2, at:at + P], combine[:, tt, e:e + 1].to_broadcast([P, P]), ident,
                                                start=True, stop=True)
                        ins.then_inc(S("comb_full"), 1)
                    ffn("exp_up", "exp_down", SEQ)
                if ph == "ple":
                    pe.wait_ge(S("h_ready"), 20)
                    panels("ple_gate", tiles(h_hi, SEQ), tiles(h_lo, SEQ))
                    pe.wait_ge(S("ple_split"), 1)
                    pl = [[R(at, 2, SEQ)[:, k] for k in range(2)] for at in (0, 512)]
                    for n in range(8):
                        if n % 4 == 0:
                            slot = ready("ple_w", 0, n // 4)
                        bank_free("ple_w", n % 4, n // 4)
                        ins = stationary(lin[:, n % 4, 0:SEQ], slot, range(2 * (n % 4), 2 * (n % 4) + 2), pl[0], pl[1], True, True)
                        if n % 4 == 3:
                            ins.then_inc(units_done, 1)

    return nc


def kernel(**inputs):
    import concourse.bacc as bacc
    from concourse.bass_utils import run_bass_kernel_spmd

    arrays = host_inputs(inputs)
    nc = bacc.Bacc("TRN2", target_bir_lowering=False, num_devices=1)
    dram = {n: nc.dram_tensor(n, a.shape, mybir.dt.from_np(a.dtype), kind="ExternalInput").ap() for n, a in arrays.items()}
    out = nc.dram_tensor("out", (P, KT, SEQ), F32, kind="ExternalOutput").ap()
    build_program(nc, dram, out)
    r = run_bass_kernel_spmd(nc, [arrays], core_ids=[0])
    y = r.results[0]["out"]
    return np.ascontiguousarray(y.transpose(2, 1, 0)).reshape(1, SEQ, D)
```
